# Optimizing a Trainium2 kernel written in Bass

```python
import math
import jax, jax.numpy as jnp
from jax import lax
import numpy as np

D_MODEL = 1024
BATCH = 1
SEQ = 256
DEPTH = 2

CHUNK = 64
Q_BLOCK = 128
N_MIXERS = 2
DIFF_HEADS = 8
DIFF_HEAD_DIM = D_MODEL // (2 * DIFF_HEADS)
SB_HEADS = 16
SB_HEAD_DIM = D_MODEL // SB_HEADS
N_GROUPS = 4
EXPERTS_PER_GROUP = 8
N_EXPERTS = N_GROUPS * EXPERTS_PER_GROUP
TOP_K = 2
EXPERT_HIDDEN = D_MODEL // 2
MOE_BLOCK = 128
RMS_EPS = 1e-6
SUBLN_EPS = 1e-5


def rms_norm(x, g, eps=RMS_EPS):
    xf = x.astype(jnp.float32)
    y = xf * lax.rsqrt(jnp.mean(xf * xf, axis=-1, keepdims=True) + eps)
    return (y * g.astype(jnp.float32)).astype(x.dtype)

def alibi_slopes(n_heads):
    return jnp.exp2(-8.0 * jnp.arange(1, n_heads + 1, dtype=jnp.float32) / n_heads)

def diff_attention(h, w_in, w_out, lq1, lk1, lq2, lk2, subln_g, lambda_init):
    B, S, D = h.shape
    H, d = DIFF_HEADS, DIFF_HEAD_DIM
    q, k, v = jnp.split(h @ w_in, 3, axis=-1)
    q = q.reshape(B, S, H, 2, d)
    k = k.reshape(B, S, H, 2, d)
    v = v.reshape(B, S, H, 2 * d)
    lam = (jnp.exp(jnp.sum(lq1.astype(jnp.float32) * lk1.astype(jnp.float32)))
           - jnp.exp(jnp.sum(lq2.astype(jnp.float32) * lk2.astype(jnp.float32)))
           + lambda_init)
    slopes = alibi_slopes(H)[None, :, None, None, None]
    scale = 1.0 / math.sqrt(d)
    pos = jnp.arange(S, dtype=jnp.int32)
    outs = []
    for i in range(S // Q_BLOCK):
        q0, q1 = i * Q_BLOCK, (i + 1) * Q_BLOCK
        qb, kb, vb = q[:, q0:q1], k[:, :q1], v[:, :q1]
        tq, tk = pos[q0:q1], pos[:q1]
        s = jnp.einsum('bqhmd,bkhmd->bhmqk', qb, kb).astype(jnp.float32) * scale
        dist = jnp.abs(tq[:, None] - tk[None, :]).astype(jnp.float32)
        allowed = (tk[None, :] // CHUNK) <= (tq[:, None] // CHUNK)
        s = jnp.where(allowed, s - slopes * dist, -jnp.inf)
        p = jax.nn.softmax(s, axis=-1)
        a = p[:, :, 0] - lam * p[:, :, 1]
        outs.append(jnp.einsum('bhqk,bkhe->bqhe', a.astype(vb.dtype), vb))
    o = jnp.concatenate(outs, axis=1)
    o = rms_norm(o, subln_g, SUBLN_EPS) * (1.0 - lambda_init)
    return o.reshape(B, S, D) @ w_out

def stick_breaking_attention(h, w_in, w_out):
    B, S, D = h.shape
    H, d = SB_HEADS, SB_HEAD_DIM
    q, k, v = jnp.split(h @ w_in, 3, axis=-1)
    q = q.reshape(B, S, H, d)
    k = k.reshape(B, S, H, d)
    v = v.reshape(B, S, H, d)
    scale = 1.0 / math.sqrt(d)
    pos = jnp.arange(S, dtype=jnp.int32)
    outs = []
    for i in range(S // Q_BLOCK):
        q0, q1 = i * Q_BLOCK, (i + 1) * Q_BLOCK
        qb, kb, vb = q[:, q0:q1], k[:, :q1], v[:, :q1]
        tq, tk = pos[q0:q1], pos[:q1]
        z = jnp.einsum('bqhd,bkhd->bhqk', qb, kb).astype(jnp.float32) * scale
        strict = tk[None, :] < tq[:, None]
        log_fail = jnp.where(strict, jax.nn.log_sigmoid(-z), 0.0)
        between = lax.cumsum(log_fail, axis=log_fail.ndim - 1, reverse=True) - log_fail
        a = jnp.where(strict, jnp.exp(jax.nn.log_sigmoid(z) + between), 0.0)
        outs.append(jnp.einsum('bhqk,bkhd->bqhd', a.astype(vb.dtype), vb))
    o = jnp.concatenate(outs, axis=1)
    return o.reshape(B, S, D) @ w_out

def expert_dispatch(xf, expert_ids, weights, w_gate, w_up, w_down):
    N, D = xf.shape
    NK = expert_ids.shape[0]
    n_slots = NK + N_EXPERTS * MOE_BLOCK
    n_blocks = n_slots // MOE_BLOCK
    token_ids = jnp.arange(NK, dtype=jnp.int32) // TOP_K
    order = jnp.argsort(expert_ids)
    e_sorted = expert_ids[order]
    counts = jnp.zeros((N_EXPERTS,), jnp.int32).at[expert_ids].add(1)
    padded = (counts + MOE_BLOCK - 1) // MOE_BLOCK * MOE_BLOCK
    starts = jnp.cumsum(counts) - counts
    pad_ends = jnp.cumsum(padded)
    pad_starts = pad_ends - padded
    rank = jnp.arange(NK, dtype=jnp.int32) - starts[e_sorted]
    dest = pad_starts[e_sorted] + rank
    slot_tok = jnp.full((n_slots,), N, jnp.int32).at[dest].set(token_ids[order])
    slot_w = jnp.zeros((n_slots,), jnp.float32).at[dest].set(weights[order])
    block_start = jnp.arange(n_blocks, dtype=jnp.int32) * MOE_BLOCK
    block_expert = jnp.minimum(jnp.searchsorted(pad_ends, block_start, side='right'),
                               N_EXPERTS - 1).astype(jnp.int32)
    x_pad = jnp.concatenate([xf, jnp.zeros((1, D), xf.dtype)], axis=0)
    xs = x_pad[slot_tok].reshape(n_blocks, MOE_BLOCK, D)

    def run_block(args):
        xb, e = args
        hid = jax.nn.silu(xb @ w_gate[e]) * (xb @ w_up[e])
        return hid @ w_down[e]

    ys = lax.map(run_block, (xs, block_expert)).reshape(n_slots, D)
    ys = ys * slot_w[:, None].astype(ys.dtype)
    out = jnp.zeros((N + 1, D), ys.dtype).at[slot_tok].add(ys)
    return out[:N]

def hierarchical_moe(h, w_group, b_group, w_expert, b_expert, w_gate, w_up, w_down):
    B, S, D = h.shape
    N = B * S
    xf = h.reshape(N, D)
    rows = jnp.arange(N, dtype=jnp.int32)
    g_logits = (xf @ w_group).astype(jnp.float32) + b_group.astype(jnp.float32)
    g_prob = jax.nn.softmax(g_logits, axis=-1)
    g_idx = jnp.argmax(g_logits, axis=-1).astype(jnp.int32)
    g_w = g_prob[rows, g_idx][:, None]
    e_all = ((xf @ w_expert).astype(jnp.float32).reshape(N, N_GROUPS, EXPERTS_PER_GROUP)
             + b_expert.astype(jnp.float32))
    e_logits = e_all[rows, g_idx]
    top_v, top_i = lax.top_k(e_logits, TOP_K)
    e_w = jax.nn.softmax(top_v, axis=-1)
    weights = (g_w * e_w).reshape(-1)
    expert_ids = (g_idx[:, None] * EXPERTS_PER_GROUP + top_i.astype(jnp.int32)).reshape(-1)
    y = expert_dispatch(xf, expert_ids, weights, w_gate, w_up, w_down)
    return y.reshape(B, S, D)

def first_inputs(seed: int = 0) -> dict:
    key = jax.random.key(seed)
    ks = jax.random.split(key, 24)
    D, F, E = D_MODEL, EXPERT_HIDDEN, N_EXPERTS
    nA = (DEPTH + 1) // 2
    nB = DEPTH // 2
    dA = DIFF_HEAD_DIM
    nrm = jax.random.normal
    f32 = jnp.float32
    inv = D ** -0.5
    return {
        "x": nrm(ks[0], (BATCH, SEQ, D), f32),
        "c": nrm(ks[1], (BATCH, D), f32),
        "norm1_g": 1.0 + 0.02 * nrm(ks[2], (DEPTH, D), f32),
        "norm2_g": 1.0 + 0.02 * nrm(ks[3], (DEPTH, D), f32),
        "ada_w": 0.5 * inv * nrm(ks[4], (DEPTH, D, 6 * D), f32),
        "ada_b": 0.01 * nrm(ks[5], (DEPTH, 6 * D), f32),
        "diff_w_in": inv * nrm(ks[6], (nA, D, 3 * D), f32),
        "diff_w_out": inv * nrm(ks[7], (nA, D, D), f32),
        "diff_lambda_q1": 0.1 * nrm(ks[8], (nA, dA), f32),
        "diff_lambda_k1": 0.1 * nrm(ks[9], (nA, dA), f32),
        "diff_lambda_q2": 0.1 * nrm(ks[10], (nA, dA), f32),
        "diff_lambda_k2": 0.1 * nrm(ks[11], (nA, dA), f32),
        "diff_subln_g": 1.0 + 0.02 * nrm(ks[12], (nA, 2 * dA), f32),
        "sb_w_in": inv * nrm(ks[13], (nB, D, 3 * D), f32),
        "sb_w_out": inv * nrm(ks[14], (nB, D, D), f32),
        "router_group_w": inv * nrm(ks[15], (DEPTH, D, N_GROUPS), f32),
        "router_group_b": 0.01 * nrm(ks[16], (DEPTH, N_GROUPS), f32),
        "router_expert_w": inv * nrm(ks[17], (DEPTH, D, N_GROUPS * EXPERTS_PER_GROUP), f32),
        "router_expert_b": 0.01 * nrm(ks[18], (DEPTH, N_GROUPS, EXPERTS_PER_GROUP), f32),
        "expert_w_gate": inv * nrm(ks[19], (DEPTH, E, D, F), f32),
        "expert_w_up": inv * nrm(ks[20], (DEPTH, E, D, F), f32),
        "expert_w_down": (F ** -0.5) * nrm(ks[21], (DEPTH, E, F, D), f32),
        "final_norm_g": 1.0 + 0.02 * nrm(ks[22], (D,), f32),
    }

def first_block(x, c, norm1_g, norm2_g, ada_w, ada_b, diff_w_in, diff_w_out,
              diff_lambda_q1, diff_lambda_k1, diff_lambda_q2, diff_lambda_k2, diff_subln_g,
              sb_w_in, sb_w_out, router_group_w, router_group_b, router_expert_w,
              router_expert_b, expert_w_gate, expert_w_up, expert_w_down, final_norm_g):
    cond = jax.nn.silu(c)
    for i in range(DEPTH):
        mod = cond @ ada_w[i] + ada_b[i]
        sh1, sc1, g1, sh2, sc2, g2 = jnp.split(mod[:, None, :], 6, axis=-1)
        h = rms_norm(x, norm1_g[i]) * (1.0 + sc1) + sh1
        j = i // N_MIXERS
        if i % N_MIXERS == 0:
            lambda_init = 0.8 - 0.6 * math.exp(-0.3 * i)
            y = diff_attention(h, diff_w_in[j], diff_w_out[j], diff_lambda_q1[j],
                               diff_lambda_k1[j], diff_lambda_q2[j], diff_lambda_k2[j],
                               diff_subln_g[j], lambda_init)
        else:
            y = stick_breaking_attention(h, sb_w_in[j], sb_w_out[j])
        x = x + g1 * y
        h = rms_norm(x, norm2_g[i]) * (1.0 + sc2) + sh2
        y = hierarchical_moe(h, router_group_w[i], router_group_b[i], router_expert_w[i],
                             router_expert_b[i], expert_w_gate[i], expert_w_up[i],
                             expert_w_down[i])
        x = x + g2 * y
    return rms_norm(x, final_norm_g)


CTX_LEN = 256
GRID_W = 64

F_GROUPS = 4
F_GROUP_DIM = D_MODEL // 16
F_WIDTH = F_GROUPS * F_GROUP_DIM
G_HEADS = 4
G_HEAD_DIM = D_MODEL // 16
G_WIDTH = G_HEADS * G_HEAD_DIM
CHUNK_2 = 128
A_HEADS = 8
A_NOPE = D_MODEL // 16
A_ROPE = D_MODEL // 32
A_V = D_MODEL // 16
A_QK = A_NOPE + A_ROPE
A_WIDTH = A_HEADS * A_V
Q_LORA = D_MODEL // 4
KV_LORA = D_MODEL // 8

MIX_WIDTH = F_WIDTH + G_WIDTH + A_WIDTH
IN_WIDTH = 2 * F_WIDTH + 3 * G_WIDTH + Q_LORA + KV_LORA + A_ROPE + A_WIDTH
ROPE_BASE = 10000.0
EPS = 1e-6


def _rmsnorm(t, g):
    tf = t.astype(jnp.float32)
    tf = tf * lax.rsqrt(jnp.mean(tf * tf, axis=-1, keepdims=True) + EPS)
    return (tf * g.astype(jnp.float32)).astype(t.dtype)

def _layernorm(t, g):
    tf = t.astype(jnp.float32)
    tf = tf - jnp.mean(tf, axis=-1, keepdims=True)
    tf = tf * lax.rsqrt(jnp.mean(tf * tf, axis=-1, keepdims=True) + EPS)
    return (tf * g.astype(jnp.float32)).astype(t.dtype)

def _split_in(p):
    sizes = (F_WIDTH, F_WIDTH, G_WIDTH, G_WIDTH, G_WIDTH, Q_LORA, KV_LORA, A_ROPE, A_WIDTH)
    parts = []
    start = 0
    for s in sizes:
        parts.append(p[..., start:start + s])
        start += s
    return parts

def _axial_rope(n):
    rows = n // GRID_W
    row = jnp.repeat(jnp.arange(rows, dtype=jnp.float32), GRID_W)
    col = jnp.tile(jnp.arange(GRID_W, dtype=jnp.float32), rows)
    half = A_ROPE // 2
    inv = ROPE_BASE ** (-jnp.arange(0, half, 2, dtype=jnp.float32) / half)
    ang_r = row[:, None] * inv[None, :]
    ang_c = col[:, None] * inv[None, :]
    ang = jnp.concatenate([ang_r, ang_r, ang_c, ang_c], axis=-1)
    return jnp.cos(ang), jnp.sin(ang)

def _apply_rope(t, rope):
    cos, sin = rope
    q = A_ROPE // 4
    x1, x2, x3, x4 = t[..., :q], t[..., q:2 * q], t[..., 2 * q:3 * q], t[..., 3 * q:]
    rot = jnp.concatenate([-x2, x1, -x4, x3], axis=-1)
    cos = cos[:, None, :].astype(t.dtype)
    sin = sin[:, None, :].astype(t.dtype)
    return t * cos + rot * sin

def _fourier(u):
    b, n, _ = u.shape
    ug = u.astype(jnp.float32).reshape(b, n, F_GROUPS, F_GROUP_DIM).transpose(0, 2, 1, 3)
    f = jnp.fft.fft2(ug, norm="ortho").real
    return f.transpose(0, 2, 1, 3).reshape(b, n, F_WIDTH).astype(u.dtype)

def _spatial_gate(u, v, ln_g, ws, bs):
    b, n, _ = v.shape
    vh = v.reshape(b, n // CHUNK_2, CHUNK_2, G_HEADS, G_HEAD_DIM)
    vh = _layernorm(vh, ln_g)
    mixed = jnp.einsum('hpq,bcqhd->bcphd', ws, vh) + bs.T[None, None, :, :, None]
    return u * mixed.reshape(b, n, G_WIDTH)

def _mla_qkv(c_q, c_kv, k_rope, q_a_g, w_uq, kv_a_g, w_ukv, q_norm_g, k_norm_g, rope):
    b, n, _ = c_q.shape
    q = (_rmsnorm(c_q, q_a_g) @ w_uq).reshape(b, n, A_HEADS, A_QK)
    kv = (_rmsnorm(c_kv, kv_a_g) @ w_ukv).reshape(b, n, A_HEADS, A_NOPE + A_V)
    k_nope, v = kv[..., :A_NOPE], kv[..., A_NOPE:]
    k_r = jnp.broadcast_to(k_rope[:, :, None, :], (b, n, A_HEADS, A_ROPE))
    k = jnp.concatenate([k_nope, k_r], axis=-1)
    q = _rmsnorm(q, q_norm_g)
    k = _rmsnorm(k, k_norm_g)
    if rope is not None:
        q = jnp.concatenate([q[..., :A_NOPE], _apply_rope(q[..., A_NOPE:], rope)], axis=-1)
        k = jnp.concatenate([k[..., :A_NOPE], _apply_rope(k[..., A_NOPE:], rope)], axis=-1)
    return q, k, v

def _branches(h, w_in, w_fmix, g_ln_g, g_ws, g_bs, q_a_g, w_uq, kv_a_g, w_ukv, q_norm_g, k_norm_g, rope):
    f_in, f_gate, g_u, g_v, g_gate, c_q, c_kv, k_rope, a_gate = _split_in(h @ w_in)
    f_out = (_fourier(f_in) @ w_fmix) * jax.nn.silu(f_gate)
    g_out = _spatial_gate(g_u, g_v, g_ln_g, g_ws, g_bs) * jax.nn.silu(g_gate)
    q, k, v = _mla_qkv(c_q, c_kv, k_rope, q_a_g, w_uq, kv_a_g, w_ukv, q_norm_g, k_norm_g, rope)
    return f_out, g_out, q, k, v, a_gate

def _attend(q, k, v):
    s = jnp.einsum('bqhd,bkhd->bhqk', q, k).astype(jnp.float32) * (A_QK ** -0.5)
    p = jax.nn.softmax(s, axis=-1).astype(v.dtype)
    return jnp.einsum('bhqk,bkhd->bqhd', p, v)

def _blocked_attention(q, k, v):
    b, n, h, d = q.shape
    nb = n // Q_BLOCK
    qb = q.reshape(b, nb, Q_BLOCK, h, d).transpose(1, 0, 2, 3, 4)
    o = lax.map(lambda blk: _attend(blk, k, v), qb)
    return o.transpose(1, 0, 2, 3, 4).reshape(b, n, h * A_V)

def second_inputs(seed: int = 0) -> dict:
    key = jax.random.key(seed)
    ks = jax.random.split(key, 24)
    f32 = jnp.float32
    nrm = lambda k, shape, s: jax.random.normal(k, shape, f32) * s
    gain = lambda k, shape: 1.0 + 0.02 * jax.random.normal(k, shape, f32)
    return {
        "x": nrm(ks[0], (BATCH, SEQ, D_MODEL), 1.0),
        "c": nrm(ks[1], (BATCH, D_MODEL), 1.0),
        "ctx": nrm(ks[2], (BATCH, CTX_LEN, D_MODEL), 1.0),
        "c_ctx": nrm(ks[3], (D_MODEL,), 1.0),
        "w_mod": nrm(ks[4], (DEPTH, D_MODEL, 3 * D_MODEL), 0.5 * D_MODEL ** -0.5),
        "b_mod": nrm(ks[5], (DEPTH, 3 * D_MODEL), 0.01),
        "norm_g": gain(ks[6], (DEPTH, D_MODEL)),
        "w_in": nrm(ks[7], (DEPTH, D_MODEL, IN_WIDTH), D_MODEL ** -0.5),
        "w_fmix": nrm(ks[8], (DEPTH, F_WIDTH, F_WIDTH), F_WIDTH ** -0.5),
        "g_ln_g": gain(ks[9], (DEPTH, G_HEAD_DIM)),
        "g_ws": nrm(ks[10], (DEPTH, G_HEADS, CHUNK_2, CHUNK_2), CHUNK_2 ** -0.5),
        "g_bs": 1.0 + nrm(ks[11], (DEPTH, G_HEADS, CHUNK_2), 0.01),
        "q_a_g": gain(ks[12], (DEPTH, Q_LORA)),
        "w_uq": nrm(ks[13], (DEPTH, Q_LORA, A_HEADS * A_QK), Q_LORA ** -0.5),
        "kv_a_g": gain(ks[14], (DEPTH, KV_LORA)),
        "w_ukv": nrm(ks[15], (DEPTH, KV_LORA, A_HEADS * (A_NOPE + A_V)), KV_LORA ** -0.5),
        "q_norm_g": gain(ks[16], (DEPTH, A_QK)),
        "k_norm_g": gain(ks[17], (DEPTH, A_QK)),
        "w_out": nrm(ks[18], (DEPTH, MIX_WIDTH, D_MODEL), MIX_WIDTH ** -0.5),
    }

def second_block(x, c, ctx, c_ctx, w_mod, b_mod, norm_g, w_in, w_fmix, g_ln_g, g_ws, g_bs,
              q_a_g, w_uq, kv_a_g, w_ukv, q_norm_g, k_norm_g, w_out):
    n = x.shape[1]
    rope = _axial_rope(n)
    y = ctx
    silu_c = jax.nn.silu(c)
    silu_cc = jax.nn.silu(c_ctx)
    for l in range(DEPTH):
        shift, scale, gate = jnp.split(silu_c @ w_mod[l] + b_mod[l], 3, axis=-1)
        shift_c, scale_c, gate_c = jnp.split(silu_cc @ w_mod[l] + b_mod[l], 3, axis=-1)
        hx = _rmsnorm(x, norm_g[l]) * (1.0 + scale[:, None, :]) + shift[:, None, :]
        hy = _rmsnorm(y, norm_g[l]) * (1.0 + scale_c) + shift_c
        params = (w_in[l], w_fmix[l], g_ln_g[l], g_ws[l], g_bs[l], q_a_g[l], w_uq[l],
                  kv_a_g[l], w_ukv[l], q_norm_g[l], k_norm_g[l])
        fy, gy, qy, ky, vy, ay = _branches(hy, *params, None)
        fx, gx, qx, kx, vx, ax = _branches(hx, *params, rope)
        k_all = jnp.concatenate([ky, kx], axis=1)
        v_all = jnp.concatenate([vy, vx], axis=1)
        ox = _blocked_attention(qx, k_all, v_all) * jax.nn.silu(ax)
        x = x + gate[:, None, :] * (jnp.concatenate([fx, gx, ox], axis=-1) @ w_out[l])
        if l < DEPTH - 1:
            b = y.shape[0]
            oy = _attend(qy, ky, vy).reshape(b, y.shape[1], A_WIDTH) * jax.nn.silu(ay)
            y = y + gate_c * (jnp.concatenate([fy, gy, oy], axis=-1) @ w_out[l])
    return x


def setup_inputs(seed=0):
    out = dict(first_inputs(seed))
    for name, value in second_inputs(seed + 1).items():
        if name != "x":
            out[name + "_2"] = value
    return out


def reference(
    x, c, norm1_g, norm2_g, ada_w, ada_b, diff_w_in, diff_w_out, diff_lambda_q1, diff_lambda_k1,
    diff_lambda_q2, diff_lambda_k2, diff_subln_g, sb_w_in, sb_w_out, router_group_w,
    router_group_b, router_expert_w, router_expert_b, expert_w_gate, expert_w_up, expert_w_down,
    final_norm_g, c_2, ctx_2, c_ctx_2, w_mod_2, b_mod_2, norm_g_2, w_in_2, w_fmix_2, g_ln_g_2,
    g_ws_2, g_bs_2, q_a_g_2, w_uq_2, kv_a_g_2, w_ukv_2, q_norm_g_2, k_norm_g_2, w_out_2,
):
    x = first_block(
        x, c, norm1_g, norm2_g, ada_w, ada_b, diff_w_in, diff_w_out, diff_lambda_q1,
        diff_lambda_k1, diff_lambda_q2, diff_lambda_k2, diff_subln_g, sb_w_in, sb_w_out,
        router_group_w, router_group_b, router_expert_w, router_expert_b, expert_w_gate,
        expert_w_up, expert_w_down, final_norm_g,
    )
    return second_block(
        x, c_2, ctx_2, c_ctx_2, w_mod_2, b_mod_2, norm_g_2, w_in_2, w_fmix_2, g_ln_g_2, g_ws_2,
        g_bs_2, q_a_g_2, w_uq_2, kv_a_g_2, w_ukv_2, q_norm_g_2, k_norm_g_2, w_out_2,
    )


_drawn_inputs = setup_inputs


def setup_inputs(seed=0):
    import zlib

    import numpy as np

    out = dict(_drawn_inputs(seed))
    spreads = {}
    factors = {'norm1_g': 4.693,
     'norm2_g': 3.53,
     'diff_lambda_k1': 8.0,
     'diff_lambda_q2': 8.0,
     'diff_subln_g': 5.337,
     'router_group_b': 7.454,
     'router_expert_b': 5.4,
     'final_norm_g': 2.733,
     'ctx_2': 6.105,
     'b_mod_2': 6.091,
     'norm_g_2': 7.726,
     'g_ln_g_2': 8.0,
     'g_bs_2': 8.0,
     'q_a_g_2': 8.0,
     'w_uq_2': 2.834,
     'kv_a_g_2': 8.0,
     'q_norm_g_2': 8.0,
     'k_norm_g_2': 8.0}
    for name, (base, spread) in spreads.items():
        noise = np.random.default_rng([zlib.crc32(name.encode()), seed]).standard_normal(out[name].shape)
        drawn = base * np.exp(spread * noise) if base else spread * noise
        out[name] = __import__('jax').numpy.asarray(drawn.astype(out[name].dtype))
    for name, factor in factors.items():
        out[name] = (out[name] * factor).astype(out[name].dtype)
    return out
```

```python
from contextlib import ExitStack

import concourse.bass as bass
import numpy as np
from concourse import mybir

F32 = mybir.dt.float32
I32 = mybir.dt.int32
ALU = mybir.AluOpType
ACT = mybir.ActivationFunctionType
AX = mybir.AxisListType

P = 128
D = 1024
S = 256
TT = S // P
KT = D // P
HEADS_D = 8
HEADS_S = 16
HD = 64
NG, NE = 4, 8
NX = NG * NE
FH = 512
FK = FH // P
RING = 6
SLOT = KT * 512
UC = 6 * D // NX
NBIG = -1e30
A_HEADS, A_QK, A_NOPE, A_ROPE, A_V = 8, 96, 64, 32, 64
IN_W = 2208
WORK = 19200

EACH = dict(qkv_mm=12, qkv=12, proj_mm=4, oT=4, y_mm=4, hover_mm=1, hover=2, wsl_mm=1, wsl=1, cnt=1, gather_mm=NG, hcur=2 * NG,
            gu=NX, silu=NX, hid=NX, hid_tr=NX, hidT=NX, group_mm=NG, acc=2 * NG, selT_mm=3, selT=3, sel=TT, logits=1, og=1,
            rank_mm=1, gdiff=1, ediff=1, r_exp=2, over_zero=1)
EACH.update({n: 2 * A_HEADS * TT for n in ("a_s", "a_max", "a_exp", "a_tr", "a_pT", "a_pv", "a_o")})
EACH.update({n: 4 * TT for n in ("tok", "u_mm", "u_ss", "u_rms", "u_n", "u_tr", "uT")})
EACH.update(rms2=1, h2=2 * TT, h2T_mm=KT, h2T=KT, in_mm=10 * TT, proj=10 * TT, c_ss=1, c_rms=1, c_n=2 * TT, c_mm=1, cT=1,
            v_ss=1, v_rms=1, v_n=2 * TT, ws_mm=1, wsT=1, fa_mm=2, fa=2, ft_mm=2, ft=2, fm_mm=2, f_out=2, sg_mm=1, g_out=1,
            mixT_mm=8, mixT=8, out_mm=4 * TT, out_used=4 * TT - 1)

CONST_COLS = (("ident", P), ("suffix", P), ("minus", P), ("ones", P), ("before", P), ("iota", P), ("iota_over", P),
              ("dist0", P), ("dist1", S), ("strict", 3 * P), ("prio4", NG), ("prio8", NE))
CONST_W = sum(w for _, w in CONST_COLS)
CONST2_COLS = (("rope_cos", TT * A_ROPE), ("rope_sin", TT * A_ROPE), ("dft_cos", TT * S), ("dft_sin", TT * S),
               ("grp_cos", P), ("grp_sin", P))
CONST2_W = sum(w for _, w in CONST2_COLS)


def constants():
    i, j = np.arange(P)[:, None], np.arange(P)[None, :]
    k = np.arange(S)[None, :]

    def dist(q, k):
        return np.where(k // 64 <= q // 64, -np.abs(q - k), NBIG)

    strict = np.concatenate([j > i, np.ones((P, P)), j > i], 1)
    row = np.ones((P, 1))
    parts = dict(ident=i == j, suffix=-(i >= j).astype(float), minus=-np.ones((P, P)), ones=np.ones((P, P)), before=i < j,
                 iota=row * j, iota_over=row * (j + P), dist0=dist(i, j), dist1=dist(i + P, k), strict=strict,
                 prio4=row * (NG - np.arange(NG)), prio8=row * (NE - np.arange(NE)))
    first = np.concatenate([np.asarray(parts[n], np.float32) for n, _ in CONST_COLS], 1)
    pos = np.arange(S)
    half = A_ROPE // 2
    inv = (np.float32(10000.0) ** (-np.arange(0, half, 2, dtype=np.float32) / np.float32(half))).astype(np.float32)
    ar, ac = (pos // 64).astype(np.float32)[:, None] * inv, (pos % 64).astype(np.float32)[:, None] * inv
    ang = np.concatenate([ar, ar, ac, ac], 1)
    sign = np.repeat([-1.0, 1.0, -1.0, 1.0], A_ROPE // 4)
    tok = lambda a: np.asarray(a).reshape(TT, P, -1).transpose(1, 0, 2).reshape(P, -1)
    th = 2 * np.pi * ((pos[:, None] * pos[None, :]) % S) / S
    f = np.arange(HD)
    tf = 2 * np.pi * ((f[:, None] * f[None, :]) % HD) / HD
    scale = 1.0 / np.sqrt(S * HD)
    two = np.eye(2)
    second = np.concatenate([tok(np.cos(ang)), tok(np.sin(ang) * sign), tok(np.cos(th)), tok(np.sin(th)),
                             np.kron(two, np.cos(tf)) * scale, -np.kron(two, np.sin(tf)) * scale], 1)
    return {"consts": first.astype(np.float32), "consts2": second.astype(np.float32)}


class Chain:

    def __init__(self, eng, sem):
        self.eng, self.sem, self.n = eng, sem, 0

    def __call__(self, ins):
        self.n += 1
        ins.then_inc(self.sem, 1)
        self.eng.wait_ge(self.sem, self.n)


def build(nc, a, out, dbg=None, parts=("first", "second")):
    ctx = ExitStack()
    sb = lambda name, shape, dt=F32: ctx.enter_context(nc.sbuf_tensor(name, shape, dt))
    sems = {}

    def sem(name):
        if name not in sems:
            sems[name] = ctx.enter_context(nc.semaphore(name))
        return sems[name]

    with ctx:
        program(nc, a, out, sb, sem, ctx, dbg or {}, parts)


def program(nc, a, out, sb, sem, ctx, dbg, parts):
    ring = sb("ring", [P, RING, SLOT])
    cst = sb("cst", [P, CONST_W])
    x = sb("x", [P, TT, D])
    rows = sb("rows", [P, 5, D])
    work = sb("work", [P, WORK])
    small = sb("small", [P, 512])
    cnt = sb("cnt", [1, 8], I32)
    psum = ctx.enter_context(nc.psum_tensor("psum", [P, 8, 512], F32))
    bank = [psum[:, i, :] for i in range(8)]
    mod = nc.dram_tensor("mod_scratch", (24, D), F32, kind="Internal").ap()
    modf = mod.rearrange("r (o n) -> o (r n)", o=1)

    C, at = {}, 0
    for name, w in CONST_COLS:
        C[name] = cst[:, at:at + w]
        at += w
    ident = C["ident"]
    hide = cst[:, 7 * P:10 * P]

    class Carver:

        def __init__(self, start=0):
            self.at = start

        def __call__(self, *shape):
            n = int(np.prod(shape))
            v = work[:, self.at:self.at + n]
            self.at += n
            assert self.at <= WORK, self.at
            names = "abcd"[:len(shape)]
            if len(shape) == 1:
                return v
            return v.rearrange(f"p ({' '.join(names)}) -> p {' '.join(names)}", **dict(zip(names[1:], shape[1:])))

    carve = Carver()
    ada_w = carve(2, KT * UC)
    ada_prod = carve(KT * UC)
    ada_acc = carve(2, 2 * UC)
    ada_row = carve(2, 2 * UC)
    ada_bias = carve(2, UC)
    base = carve.at
    cond = small[:, 0:24].rearrange("p (c t) -> p c t", c=3)
    ss = small[:, 24:26]
    rstd = small[:, 26:28]
    lam = small[:, 28:29]
    lvec = small[:, 32:40]

    carve = Carver(base)
    h = carve(TT, D)
    hT = carve(KT, S)
    qT = carve(KT, S)
    kT = carve(KT, S)
    v = carve(TT, D)
    att = carve.at
    oT = hT
    o = h
    sc_ = carve(2, 2, S)
    pr = sc_
    aw = carve(2, S)
    awT = carve(2, 2, P)
    lqk = carve(4, HD)
    sub_g = carve(P)
    carve = Carver(att)
    sb_t = carve(2, 384)
    sb_e = sb_t
    sb_sp = carve(2, 384)
    sb_a = carve(2, 384)
    carve = Carver(base + TT * D)
    acc = carve(NG + 1, D)
    sel = carve(TT, NG + 1, P)
    selT_at = carve.at
    hcur = carve(KT, P)
    hover = carve(KT, P)
    selT = Carver(selT_at)(NG + 1, S)
    s_act = carve(FH)
    hid = carve(FH)
    hidT = carve(FK, P)
    wsl = carve(2 * NX)
    carve = Carver(base + TT * D + 2 * D)
    r_g = carve(KT, NG)
    r_e = carve(KT, NX)
    r_b = carve(NG + NX)
    rt = carve(640)

    class Cut:
        def __init__(self):
            self.at = 0

        def __call__(self, *shape):
            n = int(np.prod(shape))
            t = rt[:, self.at:self.at + n]
            self.at += n
            names = "abc"[:len(shape)]
            return t if len(shape) == 1 else t.rearrange(f"p ({' '.join(names)}) -> p {' '.join(names)}",
                                                         **dict(zip(names[1:], shape[1:])))

    cut = Cut()
    g4, g4b, g4c, og, eg = (cut(TT, NG) for _ in range(5))
    e32, e32b, w32 = (cut(TT, NX) for _ in range(3))
    e8, e8b, o1, o2, t8 = (cut(TT, NE) for _ in range(5))
    gm, pm, gs, m1, m2, ex, den, w1, w2, rk = (cut(TT) for _ in range(10))
    ogs = cut(NG)
    rkt = cut(TT, NG)

    loads = ["diff_w_in"] * 6 + ["diff_w_out"] * 2, ["sb_w_in"] * 6 + ["sb_w_out"] * 2
    L_BASE = [0, 8 + 3 * NX]
    M_BASE = [8, 16 + 3 * NX]

    def slot(n):
        return n % RING

    def loaded(eng, n, g=None):
        eng.wait_ge(sem(f"loaded{slot(n)}"), 16 * (n // RING + 1) if g is None else (n // RING + 1) * 16 + g * 64)

    def free(n):
        return sem(f"used{slot(n)}")

    def wslot(n, rows_, cols):
        return ring[:, slot(n), :].rearrange("p (t n) -> p t n", t=rows_)[:, :, 0:cols] if cols else None

    TWO = "second" in parts
    block = ctx.enter_context(nc.Block())

    ST = 2 * TT
    SECTIONS = {"f": (0, 512), "gv": (512, 512), "gq": (1024, 512), "kv": (1536, 160), "a": (1696, 512)}
    ORDER = ("gq", "kv", "f", "gv", "a")
    tail = ring[:, 3:RING, :].rearrange("p r n -> p (r n)")
    t_at = [0]

    def cut2(*shape):
        n = int(np.prod(shape))
        t = tail[:, t_at[0]:t_at[0] + n]
        t_at[0] += n
        assert t_at[0] <= 3 * SLOT
        names = "abc"[:len(shape)]
        return t if len(shape) == 1 else t.rearrange(f"p ({' '.join(names)}) -> p {' '.join(names)}",
                                                     **dict(zip(names[1:], shape[1:])))

    y = cut2(TT, D)
    cst2 = cut2(CONST2_W)
    w_uq, w_ukv, w_fm, w_gs = cut2(2, 768), cut2(1024), cut2(2, 256), cut2(4, P)
    qa_g, kva_g, qn_g, kn_g, ln_g = cut2(256), cut2(P), cut2(A_QK), cut2(A_QK), cut2(HD)
    kT2 = cut2(A_HEADS, 2 * S)
    h2 = kT2.rearrange("p a b -> p (a b)").rearrange("p (t d) -> p t d", t=ST)
    carve = Carver(0)
    hT2 = carve(KT, 2 * S)
    proj = carve(ST, IN_W)
    qT2 = carve(A_HEADS, 2 * S)
    v2 = carve(ST, A_HEADS, A_V)
    rows_y = qT2.rearrange("p a b -> p (a b)")[:, 0:2 * D].rearrange("p (r d) -> p r d", r=2)
    mixT = hT2
    hflat = hT2.rearrange("p a b -> p (a b)")
    cqT = hflat[:, 0:1024].rearrange("p (c s) -> p c s", c=2)
    ckvT = hflat[:, 1024:1536]
    tok = hflat[:, 1536:3072].rearrange("p (b h e) -> p b h e", b=2, h=A_HEADS)
    sqr = hflat[:, 3072:3840].rearrange("p (h e) -> p h e", h=A_HEADS)
    rot = hflat[:, 3840:4096].rearrange("p (h e) -> p h e", h=A_HEADS)
    pe_ = hflat[:, 0:1024].rearrange("p (b k) -> p b k", b=2)
    pT = hflat[:, 1024:2048].rearrange("p (b k q) -> p b k q", b=2, q=P)
    FT = rows[:, 0, 0:512].rearrange("p (c s) -> p c s", c=2)
    wsT = rows[:, 1, 0:512].rearrange("p (h q) -> p h q", h=4)
    AT = rows[:, 3, :].rearrange("p (k c s) -> p k c s", k=2, c=2)
    C2, at = {}, 0
    for name, w in CONST2_COLS:
        C2[name] = cst2[:, at:at + w]
        at += w
    rope_c = C2["rope_cos"].rearrange("p (t e) -> p t e", t=TT)
    rope_s = C2["rope_sin"].rearrange("p (t e) -> p t e", t=TT)
    dft = [C2[n_].rearrange("p (t s) -> p t s", t=TT) for n_ in ("dft_cos", "dft_sin")]
    ss2, rs2 = small[:, 100:104], small[:, 104:108]
    ssc, rsc = small[:, 108:116], small[:, 116:124]
    ssh, rsh = small[:, 124:132], small[:, 132:140]
    bs = small[:, 140:144]
    bsr = small[0:4, 144:272]
    lm, lr = small[:, 272:288], small[:, 288:304]
    nm2, sm2, ri2 = small[:, 304:306], small[:, 306:308], small[:, 308:310]
    stream = lambda i: y[:, i, :] if i < TT else x[:, i - TT, :]

    def fills(l):
        return [(s_, i) for s_ in ORDER for i in range(ST) if l == 0 or i >= TT or s_ == "kv"]

    def fills_through(l, s_):
        return max(n for n, f in enumerate(fills(l)) if f[0] == s_) + 1

    def out_fills(l):
        return [(hf, i) for hf in range(2) for i in range(0 if l == 0 else TT, ST)]

    def weights2():
        r = []
        for l in range(2):
            r += [(l, s_, "in_mm", EACH["in_mm"] * l + fills_through(l, s_)) for s_ in ORDER]
            r += [(l, hf, "out_mm", EACH["out_mm"] * l + len(out_fills(l)) // 2 * (hf + 1)) for hf in range(2)]
        return r

    def units(l):
        return [(k, i) for i in range(ST) for k in range(2) if not (l and k and i < TT)]

    def attn(l):
        return [(s_, hd, qt) for s_ in range(l, 2) for hd in range(A_HEADS) for qt in range(TT)]

    def sp_second(sp):
        sp.wait_ge(sem("y_mm"), 8)
        for n, (l, what, _, _) in enumerate(weights2()):
            if n >= 3:
                _, _, s_, val = weights2()[n - 3]
                sp.wait_ge(sem(s_), val)
            if isinstance(what, str):
                c0, w = SECTIONS[what]
                src = a["w_in_2"][l][:, c0:c0 + w].rearrange("(p t) n -> p t n", t=KT)
            else:
                w = 512
                src = a["w_out_2"][l][:, what * 512:(what + 1) * 512].rearrange("(t p) n -> p t n", t=KT)
            sp.dma_start(ring[:, n % 3, 0:KT * w].rearrange("p (t n) -> p t n", t=KT), src).then_inc(sem(f"in2_{n % 3}"), 16)
        sp.wait_ge(sem("x2_done"), 2)
        sp.dma_start(out[0].rearrange("(t p) d -> p t d", p=P), x[:]).then_inc(sem("out"), 16)
        sp.wait_ge(sem("out"), 16)

    def pool_second(pool):
        def get(dst, src, s_):
            pool.dma_start(dst, src).then_inc(sem(s_), 16)

        def small_weights(l):
            get(w_uq, a["w_uq_2"][l].rearrange("(c p) n -> p c n", p=P), "small_in")
            get(w_ukv, a["w_ukv_2"][l], "small_in")
            get(w_fm, a["w_fmix_2"][l].rearrange("(c p) n -> p c n", p=P), "small_in")
            get(w_gs, a["g_ws_2"][l].rearrange("h p q -> p h q"), "small_in")
            get(bsr, a["g_bs_2"][l], "small_in")
            for t_, name in ((qa_g, "q_a_g_2"), (kva_g, "kv_a_g_2"), (qn_g, "q_norm_g_2"), (kn_g, "k_norm_g_2"),
                             (ln_g, "g_ln_g_2")):
                get(t_, a[name][l:l + 1, :].to_broadcast((P, a[name].shape[1])), "small_in")

        def row(k, l, r):
            n = 12 + k * 6 + l * 3 + r
            return mod[n:n + 1, :].to_broadcast((P, D))

        pool.wait_ge(sem("y_mm"), 8)
        get(y, a["ctx_2"][0].rearrange("(t p) d -> p t d", p=P), "y_in")
        get(cst2, a["consts2"], "small_in")
        for l in range(2):
            if l:
                pool.wait_ge(sem("x2_done"), 1)
            else:
                small_weights(0)
                pool.wait_ge(sem("x_done"), 4)
            get(rows_y[:, 0, :], row(1, l, 1), "rows2_in")
            get(rows_y[:, 1, :], row(1, l, 0), "rows2_in")
            get(rows[:, 0, :], row(0, l, 1), "rows2_in")
            get(rows[:, 1, :], row(0, l, 0), "rows2_in")
            get(rows[:, 2, :], row(0, l, 2), "rows2_in")
            get(rows[:, 4, :], row(1, l, 2), "rows2_in")
            pool.wait_ge(sem("final"), 1)
            get(rows[:, 3, :], a["norm_g_2"][l:l + 1, :].to_broadcast((P, D)), "rows2_in")
            if l:
                small_weights(1)

    def act_second(act, link, copy):
        def sqrt(dst, src, n, done):
            nc.scalar.activation(dst, src, ACT.Sqrt, scale=1.0 / n, bias=small[:, 40:41]).then_inc(sem(done), 1)

        for l in range(2):
            if l == 0:
                act.wait_ge(sem("y_in"), 16)
                act.wait_ge(sem("final"), 1)
            else:
                act.wait_ge(sem("x2_done"), 1)
            for i in range(ST):
                link(nc.scalar.activation(h2[:, i, :], stream(i), ACT.Square, accum_out=ss2[:, i:i + 1]))
            sqrt(rs2, ss2, D, "rms2")
            for t in range(KT):
                act.wait_ge(sem("h2T_mm"), EACH["h2T_mm"] * l + t + 1)
                copy(hT2[:, t, :], bank[t]).then_inc(sem("h2T"), 1)
            for n, (s_, i) in enumerate(fills(l)):
                act.wait_ge(sem("in_mm"), EACH["in_mm"] * l + n + 1)
                c0, w = SECTIONS[s_]
                src = bank[n % 4]
                half = w // 2
                if s_ == "a":
                    ins = nc.scalar.activation(proj[:, i, c0:c0 + w], src, ACT.Silu)
                elif s_ in ("f", "gq"):
                    lo = s_ == "gq"
                    link(nc.scalar.activation(proj[:, i, c0:c0 + half], src[:, 0:half], ACT.Silu if lo else ACT.Copy))
                    ins = nc.scalar.activation(proj[:, i, c0 + half:c0 + w], src[:, half:w], ACT.Copy if lo else ACT.Silu)
                else:
                    ins = copy(proj[:, i, c0:c0 + w], src[:, 0:w])
                ins.then_inc(sem("proj"), 1)
            act.wait_ge(sem("c_ss"), EACH["c_ss"] * l + 1)
            link(nc.scalar.activation(rsc[:, 0:4], ssc[:, 0:4], ACT.Sqrt, scale=1.0 / 256, bias=small[:, 40:41]))
            sqrt(rsc[:, 4:8], ssc[:, 4:8], P, "c_rms")
            act.wait_ge(sem("v_ss"), EACH["v_ss"] * l + 1)
            sqrt(lr, lr, HD, "v_rms")
            act.wait_ge(sem("c_mm"), EACH["c_mm"] * l + 1)
            for c in range(2):
                link(copy(cqT[:, c, :], bank[c]))
            copy(ckvT, bank[2]).then_inc(sem("cT"), 1)
            for n, (k, i) in enumerate(units(l)):
                b = 2 * (n % 2)
                act.wait_ge(sem("u_mm"), EACH["u_mm"] * l + n + 1)
                if k:
                    src = psum[:, b:b + 2, 0:384].rearrange("p b (h e) -> p (b h) e", e=A_QK) if False else None
                    for j in range(2):
                        ins = copy(tok[:, n % 2, 4 * j:4 * j + 4, :],
                                   bank[b + j][:, 0:384].rearrange("p (h e) -> p h e", h=4))
                        if j == 0:
                            link(ins)
                else:
                    for j in range(2):
                        kv = bank[b + j].rearrange("p (h e) -> p h e", h=4)
                        link(copy(tok[:, n % 2, 4 * j:4 * j + 4, 0:A_NOPE], kv[:, :, 0:A_NOPE]))
                        link(copy(v2[:, i, 4 * j:4 * j + 4, :], kv[:, :, A_NOPE:]))
                    ins = copy(tok[:, n % 2, :, A_NOPE:], proj[:, i, 1664:1696].unsqueeze(1).to_broadcast((P, A_HEADS, A_ROPE)))
                ins.then_inc(sem("tok"), 1)
                act.wait_ge(sem("u_ss"), EACH["u_ss"] * l + n + 1)
                sqrt(rsh, ssh, A_QK, "u_rms")
                act.wait_ge(sem("u_tr"), EACH["u_tr"] * l + n + 1)
                dst = (kT2, qT2)[k]
                for j in range(2):
                    ins = copy(dst[0:A_QK, 4 * j:4 * j + 4, i * P:(i + 1) * P],
                               bank[4 + j][0:A_QK, :].rearrange("p (h s) -> p h s", h=4))
                    if j == 0:
                        link(ins)
                ins.then_inc(sem("uT"), 1)
            act.wait_ge(sem("ws_mm"), EACH["ws_mm"] * l + 1)
            link(copy(wsT.rearrange("p h q -> p (h q)"), bank[6]))
            copy(bs, bank[7][:, 0:4]).then_inc(sem("wsT"), 1)
            for n in range(l, 2):
                act.wait_ge(sem("fa_mm"), EACH["fa_mm"] * l + n - l + 1)
                for k in range(2):
                    ins = copy(AT[:, k], bank[k].rearrange("p (c s) -> p c s", c=2))
                    if k == 0:
                        link(ins)
                ins.then_inc(sem("fa"), 1)
                act.wait_ge(sem("ft_mm"), EACH["ft_mm"] * l + n - l + 1)
                copy(FT, bank[2].rearrange("p (c s) -> p c s", c=2)).then_inc(sem("ft"), 1)
            A = attn(l)
            for k in range(len(A) + 1):
                if k < len(A):
                    nk = (k_tiles := 2 + 2 * A[k][0]) * P
                    act.wait_ge(sem("a_max"), EACH["a_max"] * l + k + 1)
                    if k >= 2:
                        act.wait_ge(sem("a_o"), EACH["a_o"] * l + k - 1)
                    nc.scalar.activation(pe_[:, k % 2, 0:nk], bank[k % 2][:, 0:nk], ACT.Exp, bias=nm2[:, k % 2:k % 2 + 1],
                                         accum_out=sm2[:, k % 2:k % 2 + 1]).then_inc(sem("a_exp"), 1)
                if k >= 1:
                    u = k - 1
                    n = 2 + 2 * A[u][0]
                    act.wait_ge(sem("a_tr"), EACH["a_tr"] * l + u + 1)
                    copy(pT[:, u % 2, 0:n, :], bank[2 + u % 2][:, 0:n * P].rearrange("p (k q) -> p k q", k=n)).then_inc(
                        sem("a_pT"), 1)
            for c in range(8):
                act.wait_ge(sem("mixT_mm"), EACH["mixT_mm"] * l + c + 1)
                lo = 0 if l == 0 else S
                copy(mixT[:, c, lo:2 * S], bank[c][:, lo:2 * S]).then_inc(sem("mixT"), 1)

    def dve_second(dve, link):
        V = nc.vector
        for l in range(2):
            dve.wait_ge(sem("rows2_in"), 16 * 7 * (l + 1))
            link(V.scalar_tensor_tensor(rows_y[:, 0, :], rows_y[:, 0, :], 1.0, rows[:, 3, :], ALU.add, ALU.mult))
            link(V.scalar_tensor_tensor(rows[:, 0, :], rows[:, 0, :], 1.0, rows[:, 3, :], ALU.add, ALU.mult))
            dve.wait_ge(sem("rms2"), EACH["rms2"] * l + 1)
            link(V.reciprocal(rs2, rs2))
            for i in range(ST):
                gain, shift = (rows_y[:, 0, :], rows_y[:, 1, :]) if i < TT else (rows[:, 0, :], rows[:, 1, :])
                link(V.scalar_tensor_tensor(h2[:, i, :], stream(i), rs2[:, i:i + 1], gain, ALU.mult, ALU.mult))
                V.tensor_tensor(h2[:, i, :], h2[:, i, :], shift, ALU.add).then_inc(sem("h2"), 1)
            dve.wait_ge(sem("h2"), EACH["h2"] * l + ST)
            dve.wait_ge(sem("small_in"), 16 * (1 + 10 * (l + 1)))
            dve.wait_ge(sem("proj"), EACH["proj"] * l + len(fills(l)))
            q0 = 0 if l == 0 else TT
            nq = ST - q0
            cq, ckv = proj[:, q0:, 1280:1536], proj[:, :, 1536:1664]
            sq = qT2.rearrange("p a b -> p (a b)")
            sq_q = sq[:, 0:nq * 256].rearrange("p (t n) -> p t n", t=nq)
            sq_k = sq[:, 1024:1536].rearrange("p (t n) -> p t n", t=ST)
            if l:
                link(V.memset(ssc[:, 0:TT], 0.0))
            link(V.tensor_tensor(sq_q, cq, cq, ALU.mult))
            link(V.tensor_reduce(ssc[:, q0:ST], sq_q, AX.X, ALU.add))
            link(V.tensor_tensor(sq_k, ckv, ckv, ALU.mult))
            V.tensor_reduce(ssc[:, 4:8], sq_k, AX.X, ALU.add).then_inc(sem("c_ss"), 1)
            gv = [proj[:, i, 768:1024].rearrange("p (h e) -> p h e", h=4) for i in range(q0, ST)]
            sq_v = [sq[:, 2048 + 256 * i:2304 + 256 * i].rearrange("p (h e) -> p h e", h=4) for i in range(nq)]
            if l:
                link(V.memset(lr, 1.0))
            for i, g_ in enumerate(gv):
                m_, r_ = lm[:, 4 * i:4 * i + 4], lr[:, 4 * i:4 * i + 4]
                link(V.tensor_reduce(m_, g_, AX.X, ALU.add))
                link(V.tensor_scalar(m_, m_, 1.0 / HD, None, ALU.mult))
                link(V.tensor_tensor(g_, g_, m_.unsqueeze(2).to_broadcast((P, 4, HD)), ALU.subtract))
                link(V.tensor_tensor(sq_v[i], g_, g_, ALU.mult))
                ins = V.tensor_reduce(r_, sq_v[i], AX.X, ALU.add)
                if i < nq - 1:
                    link(ins)
            ins.then_inc(sem("v_ss"), 1)
            dve.wait_ge(sem("c_rms"), EACH["c_rms"] * l + 1)
            link(V.reciprocal(rsc, rsc))
            for i in range(ST):
                if i >= q0:
                    link(V.scalar_tensor_tensor(proj[:, i, 1280:1536], proj[:, i, 1280:1536], rsc[:, i:i + 1], qa_g, ALU.mult, ALU.mult))
                V.scalar_tensor_tensor(proj[:, i, 1536:1664], proj[:, i, 1536:1664], rsc[:, 4 + i:5 + i], kva_g,
                                       ALU.mult, ALU.mult).then_inc(sem("c_n"), 1)
            dve.wait_ge(sem("v_rms"), EACH["v_rms"] * l + 1)
            link(V.reciprocal(lr, lr))
            for i, g_ in enumerate(gv):
                link(V.tensor_tensor(g_, g_, lr[:, 4 * i:4 * i + 4].unsqueeze(2).to_broadcast((P, 4, HD)), ALU.mult))
                V.tensor_tensor(g_, g_, ln_g.unsqueeze(1).to_broadcast((P, 4, HD)), ALU.mult).then_inc(sem("v_n"), 1)
            link(V.tensor_scalar(qn_g, qn_g, A_QK ** -0.5, None, ALU.mult))
            for n, (k, i) in enumerate(units(l)):
                t_ = tok[:, n % 2]
                dve.wait_ge(sem("tok"), EACH["tok"] * l + n + 1)
                link(V.tensor_tensor(sqr, t_, t_, ALU.mult))
                V.tensor_reduce(ssh, sqr, AX.X, ALU.add).then_inc(sem("u_ss"), 1)
                dve.wait_ge(sem("u_rms"), EACH["u_rms"] * l + n + 1)
                link(V.reciprocal(rsh, rsh))
                link(V.tensor_tensor(t_, t_, rsh.unsqueeze(2).to_broadcast((P, A_HEADS, A_QK)), ALU.mult))
                ins = V.tensor_tensor(t_, t_, (kn_g, qn_g)[k].unsqueeze(1).to_broadcast((P, A_HEADS, A_QK)), ALU.mult)
                if i >= TT:
                    link(ins)
                    r_ = t_[:, :, A_NOPE:]
                    r4 = r_.rearrange("p h (a b c) -> p h a b c", a=2, b=2)
                    o4_ = rot.rearrange("p h (a b c) -> p h a b c", a=2, b=2)
                    s4 = rope_s[:, i - TT, :].rearrange("p (a b c) -> p a b c", a=2, b=2)
                    for b in range(2):
                        for a_ in range(2):
                            link(V.tensor_tensor(o4_[:, :, a_, b, :], r4[:, :, a_, 1 - b, :],
                                                 s4[:, a_, b, :].unsqueeze(1).to_broadcast((P, A_HEADS, 8)), ALU.mult))
                    link(V.tensor_tensor(r_, r_, rope_c[:, i - TT, :].unsqueeze(1).to_broadcast((P, A_HEADS, A_ROPE)), ALU.mult))
                    ins = V.tensor_tensor(r_, r_, rot, ALU.add)
                ins.then_inc(sem("u_n"), 1)
                dve.wait_ge(sem("u_n"), EACH["u_n"] * l + n + 1)
            for s_ in range(l, 2):
                dve.wait_ge(sem("fm_mm"), EACH["fm_mm"] * l + s_ - l + 1)
                V.tensor_tensor(proj[:, 2 * s_:2 * s_ + 2, 0:256], bank[3].rearrange("p (t n) -> p t n", t=2),
                                proj[:, 2 * s_:2 * s_ + 2, 256:512], ALU.mult).then_inc(sem("f_out"), 1)
            dve.wait_ge(sem("sg_mm"), EACH["sg_mm"] * l + 1)
            for hd in range(4):
                u_ = proj[:, q0:, 512 + hd * HD:512 + (hd + 1) * HD]
                src = bank[6 + hd // 2][:, (hd % 2) * 256:(hd % 2) * 256 + nq * HD].rearrange("p (t e) -> p t e", t=nq)
                link(V.scalar_tensor_tensor(u_, src, bs[:, hd:hd + 1], u_, ALU.add, ALU.mult))
            V.tensor_tensor(proj[:, q0:, 512:768], proj[:, q0:, 512:768], proj[:, q0:, 1024:1280], ALU.mult).then_inc(
                sem("g_out"), 1)
            A = attn(l)
            for k in range(len(A) + 2):
                if k < len(A):
                    nk = (2 + 2 * A[k][0]) * P
                    dve.wait_ge(sem("a_s"), EACH["a_s"] * l + k + 1)
                    if k >= 2:
                        dve.wait_ge(sem("a_exp"), EACH["a_exp"] * l + k - 1)
                    V.tensor_reduce(nm2[:, k % 2:k % 2 + 1], bank[k % 2][:, 0:nk], AX.X, ALU.max, negate=True).then_inc(
                        sem("a_max"), 1)
                if k >= 2:
                    u = k - 2
                    s_, hd, qt = A[u]
                    dve.wait_ge(sem("a_pv"), EACH["a_pv"] * l + u + 1)
                    link(V.reciprocal(ri2[:, u % 2:u % 2 + 1], sm2[:, u % 2:u % 2 + 1]))
                    g_ = proj[:, 2 * s_ + qt, 1696 + hd * A_V:1696 + (hd + 1) * A_V]
                    V.scalar_tensor_tensor(g_, bank[4 + u % 2][:, 0:A_V], ri2[:, u % 2:u % 2 + 1], g_, ALU.mult, ALU.mult).then_inc(
                        sem("a_o"), 1)
                    dve.wait_ge(sem("a_o"), EACH["a_o"] * l + u + 1)
            tmp = qT2.rearrange("p a b -> p (a b)")
            F = out_fills(l)
            for n, (hf, i) in enumerate(F):
                dve.wait_ge(sem("out_mm"), EACH["out_mm"] * l + n + 1)
                gate = rows[:, 4 if i < TT else 2, hf * 512:(hf + 1) * 512]
                dst = stream(i)[:, hf * 512:(hf + 1) * 512]
                link(V.tensor_tensor(tmp[:, n % 8 * 512:n % 8 * 512 + 512], bank[n % 4], gate, ALU.mult))
                ins = V.tensor_tensor(dst, dst, tmp[:, n % 8 * 512:n % 8 * 512 + 512], ALU.add)
                if n < len(F) - 1:
                    ins.then_inc(sem("out_used"), 1)
            ins.then_inc(sem("x2_done"), 1)
            dve.wait_ge(sem("x2_done"), l + 1)

    def pe_second(pe, mm):
        T = nc.tensor
        for l in range(2):
            q0 = 0 if l == 0 else TT
            nq = ST - q0
            pe.wait_ge(sem("h2"), EACH["h2"] * l + ST)
            for t in range(KT):
                for i in range(ST):
                    ins = T.transpose(bank[t][:, i * P:(i + 1) * P], h2[:, i, t:D:KT], ident)
                ins.then_inc(sem("h2T_mm"), 1)
            W = weights2()
            pe.wait_ge(sem("h2T"), EACH["h2T"] * l + KT)
            for n, (s_, i) in enumerate(fills(l)):
                r = next(j for j, w in enumerate(W) if w[:2] == (l, s_))
                pe.wait_ge(sem(f"in2_{r % 3}"), 16 * (r // 3 + 1))
                if n >= 4:
                    pe.wait_ge(sem("proj"), EACH["proj"] * l + n - 3)
                w = SECTIONS[s_][1]
                wt = ring[:, r % 3, 0:KT * w].rearrange("p (t n) -> p t n", t=KT)
                for t in range(KT):
                    ins = mm(bank[n % 4][:, 0:w], hT2[:, t, i * P:(i + 1) * P], wt[:, t, :], t == 0, t == KT - 1)
                ins.then_inc(sem("in_mm"), 1)
            pe.wait_ge(sem("small_in"), 16 * (1 + 10 * (l + 1)))
            for hd in range(4):
                T.transpose(bank[6][:, hd * P:(hd + 1) * P], w_gs[:, hd, :], ident)
            T.transpose(bank[7][:, 0:4], bsr, ident[0:4, 0:4]).then_inc(sem("ws_mm"), 1)
            pe.wait_ge(sem("c_n"), EACH["c_n"] * l + ST)
            for i in range(ST):
                if i >= q0:
                    for c in range(2):
                        T.transpose(bank[c][:, i * P:(i + 1) * P], proj[:, i, 1280 + c * P:1408 + c * P], ident)
                ins = T.transpose(bank[2][:, i * P:(i + 1) * P], proj[:, i, 1536:1664], ident)
            ins.then_inc(sem("c_mm"), 1)
            pe.wait_ge(sem("cT"), EACH["cT"] * l + 1)
            U = units(l)

            def unit(n):
                k, i = U[n]
                b = 2 * (n % 2)
                if n >= 2:
                    pe.wait_ge(sem("tok"), EACH["tok"] * l + n - 1)
                for j in range(2):
                    if k:
                        for c in range(2):
                            ins = mm(bank[b + j][:, 0:384], cqT[:, c, i * P:(i + 1) * P], w_uq[:, c, j * 384:(j + 1) * 384], c == 0, c == 1)
                    else:
                        ins = mm(bank[b + j], ckvT[:, i * P:(i + 1) * P], w_ukv[:, j * 512:(j + 1) * 512], True, True)
                ins.then_inc(sem("u_mm"), 1)

            unit(0)
            for n in range(len(U)):
                if n + 1 < len(U):
                    unit(n + 1)
                pe.wait_ge(sem("u_n"), EACH["u_n"] * l + n + 1)
                if n:
                    pe.wait_ge(sem("uT"), EACH["uT"] * l + n)
                for hd in range(A_HEADS):
                    ins = T.transpose(bank[4 + hd // 4][0:A_QK, (hd % 4) * P:(hd % 4 + 1) * P], tok[:, n % 2, hd, :], ident)
                ins.then_inc(sem("u_tr"), 1)
            for s_ in range(l, 2):
                if s_ > l:
                    pe.wait_ge(sem("fa"), EACH["fa"] * l + s_ - l)
                for k in range(2):
                    for c in range(2):
                        for t in range(TT):
                            ins = mm(bank[k][:, c * S:(c + 1) * S], proj[:, 2 * s_ + t, c * P:(c + 1) * P], dft[k][:, t, :], t == 0, t == 1)
                ins.then_inc(sem("fa_mm"), 1)
                pe.wait_ge(sem("fa"), EACH["fa"] * l + s_ - l + 1)
                for c in range(2):
                    for k, g_ in enumerate(("grp_cos", "grp_sin")):
                        ins = mm(bank[2][:, c * S:(c + 1) * S], C2[g_], AT[:, k, c, :], k == 0, k == 1)
                ins.then_inc(sem("ft_mm"), 1)
                pe.wait_ge(sem("ft"), EACH["ft"] * l + s_ - l + 1)
                if s_ > l:
                    pe.wait_ge(sem("f_out"), EACH["f_out"] * l + s_ - l)
                for t in range(TT):
                    for c in range(2):
                        ins = mm(bank[3][:, t * 256:(t + 1) * 256], FT[:, c, t * P:(t + 1) * P], w_fm[:, c, :], c == 0, c == 1)
                ins.then_inc(sem("fm_mm"), 1)
            pe.wait_ge(sem("wsT"), EACH["wsT"] * l + 1)
            pe.wait_ge(sem("v_n"), EACH["v_n"] * l + nq)
            for hd in range(4):
                ins = mm(bank[6 + hd // 2][:, (hd % 2) * 256:(hd % 2) * 256 + nq * HD], wsT[:, hd, :],
                         proj[:, q0:, 768 + hd * HD:768 + (hd + 1) * HD], True, True)
            ins.then_inc(sem("sg_mm"), 1)
            pe.wait_ge(sem("uT"), EACH["uT"] * l + len(U))
            pe.wait_ge(sem("fa"), EACH["fa"] * l + 2 - l)
            A = attn(l)
            for k in range(len(A) + 2):
                if k < len(A):
                    s_, hd, qt = A[k]
                    nk = (2 + 2 * s_) * P
                    if k >= 2:
                        pe.wait_ge(sem("a_exp"), EACH["a_exp"] * l + k - 1)
                    q_ = (2 * s_ + qt) * P
                    mm(bank[k % 2][:, 0:nk], qT2[0:A_QK, hd, q_:q_ + P], kT2[0:A_QK, hd, 0:nk], True, True).then_inc(sem("a_s"), 1)
                if 1 <= k <= len(A):
                    u = k - 1
                    pe.wait_ge(sem("a_exp"), EACH["a_exp"] * l + u + 1)
                    if u >= 2:
                        pe.wait_ge(sem("a_pT"), EACH["a_pT"] * l + u - 1)
                    for j in range(2 + 2 * A[u][0]):
                        ins = T.transpose(bank[2 + u % 2][:, j * P:(j + 1) * P], pe_[:, u % 2, j * P:(j + 1) * P], ident)
                    ins.then_inc(sem("a_tr"), 1)
                if k >= 2:
                    u = k - 2
                    s_, hd, qt = A[u]
                    pe.wait_ge(sem("a_pT"), EACH["a_pT"] * l + u + 1)
                    if u >= 2:
                        pe.wait_ge(sem("a_o"), EACH["a_o"] * l + u - 1)
                    n = 2 + 2 * s_
                    for j in range(n):
                        ins = mm(bank[4 + u % 2][:, 0:A_V], pT[:, u % 2, j, :], v2[:, j, hd, :], j == 0, j == n - 1)
                    ins.then_inc(sem("a_pv"), 1)
            pe.wait_ge(sem("a_o"), EACH["a_o"] * l + len(A))
            pe.wait_ge(sem("g_out"), EACH["g_out"] * l + 1)
            pe.wait_ge(sem("f_out"), EACH["f_out"] * l + 2 - l)
            cols = [0, P, 512, 640, 1696, 1824, 1952, 2080]
            for c, col in enumerate(cols):
                for i in range(q0, ST):
                    ins = T.transpose(bank[c][:, i * P:(i + 1) * P], proj[:, i, col:col + P], ident)
                ins.then_inc(sem("mixT_mm"), 1)
            pe.wait_ge(sem("mixT"), EACH["mixT"] * l + 8)
            for n, (hf, i) in enumerate(out_fills(l)):
                r = next(j for j, w in enumerate(W) if w[0] == l and w[1] == hf and not isinstance(w[1], str))
                pe.wait_ge(sem(f"in2_{r % 3}"), 16 * (r // 3 + 1))
                if n >= 4:
                    pe.wait_ge(sem("out_used"), EACH["out_used"] * l + n - 3)
                wt = ring[:, r % 3, :].rearrange("p (t n) -> p t n", t=KT)
                for t in range(KT):
                    ins = mm(bank[n % 4], mixT[:, t, i * P:(i + 1) * P], wt[:, t, :], t == 0, t == KT - 1)
                ins.then_inc(sem("out_mm"), 1)

    @block.sync
    def _(sp):
        def room(n, g=None):
            if g is None:
                if n >= RING:
                    sp.wait_ge(free(n), n // RING)
            else:
                sp.wait_ge(free(n), n // RING + 4 * g)

        def ada_unit(u, g, first, w_ap, b_ap):
            if not first or g * NE + u >= 2:
                sp.wait_ge(sem("ada_row"), UB[0] + g * NE + u - 1)
            sp.dma_start(ada_w[:, u % 2, :].rearrange("p (t n) -> p t n", t=KT), w_ap).then_inc(sem(f"ada_in{u % 2}"), 16)
            sp.dma_start(ada_bias[0:1, u % 2, :], b_ap).then_inc(sem(f"ada_in{u % 2}"), 16)

        UB = [0]
        ada = a["ada_w"]

        def ada_src(l, u, g):
            w = ada[l].rearrange("(p t) (g n) -> p t g n", t=KT, g=NG)
            b = a["ada_b"][l:l + 1, :].rearrange("a (g n) -> a g n", g=NG)
            c = u * UC
            if isinstance(g, int):
                return w[:, :, g, c:c + UC], b[:, g, c:c + UC]
            return (w[:, :, bass.ds(g, 1), c:c + UC].rearrange("p t g n -> p t (g n)"),
                    b[:, bass.ds(g, 1), c:c + UC].rearrange("a g n -> a (g n)"))

        def ada2_src(u, g):
            l, c = u // 4, (u % 4) * UC
            w = a["w_mod_2"][l].rearrange("(p t) (g n) -> p t g n", t=KT, g=NG)
            b = a["b_mod_2"][l:l + 1, :].rearrange("a (g n) -> a g n", g=NG)
            return (w[:, :, bass.ds(g, 1), c:c + UC].rearrange("p t g n -> p t (g n)"),
                    b[:, bass.ds(g, 1), c:c + UC].rearrange("a g n -> a (g n)"))

        def weight(l, n):
            room(L_BASE[l] + n)
            W = a[loads[l][n]][0]
            if n < 6:
                src = W[:, n * 512:(n + 1) * 512].rearrange("(p t) n -> p t n", t=KT)
            else:
                src = W[:, (n - 6) * 512:(n - 5) * 512].rearrange("(t p) n -> p t n", t=KT)
            sp.dma_start(wslot(L_BASE[l] + n, KT, 512), src).then_inc(sem(f"loaded{slot(L_BASE[l] + n)}"), 16)

        sp.dma_start(cst[:], a["consts"]).then_inc(sem("consts"), 16)
        for k, name in enumerate(("c", "c_2", "c_ctx_2")):
            src = a[name] if len(a[name].shape) == 2 else a[name].rearrange("(a n) -> a n", a=1)
            sp.dma_start(cond[:, k, :], src.rearrange("a (p t) -> p (a t)", p=P)).then_inc(sem("cond_in"), 16)
        sp.dma_start(x[:], a["x"][0].rearrange("(t p) d -> p t d", p=P)).then_inc(sem("x_in"), 16)
        for g in range(NG):
            for u in range(NE):
                ada_unit(u, g, True, *ada_src(0, u, g))
                if g == NG - 1 and u >= 2:
                    weight(0, u - 2)
        for l in range(2):
            for n in range(0 if l else 6, 8):
                weight(l, n)
            UB[0] = NX * (l + 1)
            with sp.Fori(0, NG) as g:
                for e in range(NE):
                    for j, name in enumerate(("expert_w_gate", "expert_w_up", "expert_w_down")):
                        n = M_BASE[l] + 3 * e + j
                        room(n, g)
                        W = a[name][l].rearrange("(g e) k n -> g e k n", g=NG)[bass.ds(g, 1), e]
                        sp.dma_start(ring[:, slot(n), :], W.rearrange("g (p t) n -> p (g t n)", p=P)).then_inc(
                            sem(f"loaded{slot(n)}"), 16)
                    ada_unit(e, g, False, *(ada_src(1, e, g) if l == 0 else ada2_src(e, g)))
        if TWO:
            sp_second(sp)
        else:
            sp.wait_ge(sem("final"), 1)
            sp.dma_start(out[0].rearrange("(t p) d -> p t d", p=P), x[:]).then_inc(sem("out"), 16)
            sp.wait_ge(sem("out"), 16)

    @block.gpsimd
    def _(pool):
        def row_load(i, src):
            pool.dma_start(rows[:, i, :], src).then_inc(sem("rows_in"), 16)

        def store_unit(u, g, n, off, conds):
            pool.wait_ge(sem("ada_row"), n)
            for k in range(conds):
                dst = off(k)
                pool.dma_start(dst, ada_row[0:1, u % 2, k * UC:(k + 1) * UC]).then_inc(sem(f"ada_out{u % 2}"), 16)

        def first_dst(l, u, g):
            v_ = modf[:, l * 6 * D:(l + 1) * 6 * D].rearrange("o (g n) -> o g n", g=NG)
            if isinstance(g, int):
                return lambda k: v_[:, g, u * UC:(u + 1) * UC]
            return lambda k: v_[:, bass.ds(g, 1), u * UC:(u + 1) * UC].rearrange("o g n -> o (g n)")

        def second_dst(u, g):
            def off(k):
                lo = 12 * D + (k * 2 + u // 4) * 3 * D
                v_ = modf[:, lo:lo + 3 * D].rearrange("o (g n) -> o g n", g=NG)
                return v_[:, bass.ds(g, 1), (u % 4) * UC:(u % 4 + 1) * UC].rearrange("o g n -> o (g n)")
            return off

        def stage_rows(n):
            l, half = n // 2, n % 2
            for par in range(2):
                pool.wait_ge(sem(f"ada_out{par}"), 16 * 16 * (l + 1))
            if n:
                pool.wait_ge(sem("h_done"), n)
            if n >= 2:
                pool.wait_ge(sem("x_done"), n - 1)
            r = 6 * l + 3 * half
            row_load(0, mod[r + 1:r + 2, :].to_broadcast((P, D)))
            row_load(1, mod[r:r + 1, :].to_broadcast((P, D)))
            row_load(2 if half == 0 else 4, mod[r + 2:r + 3, :].to_broadcast((P, D)))
            row_load(3, a["norm2_g" if half else "norm1_g"][l:l + 1, :].to_broadcast((P, D)))

        for g in range(NG):
            for u in range(NE):
                store_unit(u, g, g * NE + u + 1, first_dst(0, u, g), 1)
        stage_rows(0)
        for k, name in enumerate(("diff_lambda_q1", "diff_lambda_k1", "diff_lambda_q2", "diff_lambda_k2")):
            pool.dma_start(lqk[:, k, :], a[name][0:1, :].to_broadcast((P, HD))).then_inc(sem("lam_in"), 16)
        pool.dma_start(sub_g, a["diff_subln_g"][0:1, :].to_broadcast((P, P))).then_inc(sem("lam_in"), 16)
        for l in range(2):
            if l:
                stage_rows(2)
            stage_rows(2 * l + 1)
            pool.wait_ge(sem("x_done"), 2 * l + 1)
            if dbg: pool.dma_start(dbg["x"][l].rearrange("(t p) d -> p t d", p=P), x[:]).then_inc(sem("dbg"), 16)
            pool.dma_start(r_g, a["router_group_w"][l].rearrange("(p t) n -> p t n", t=KT)).then_inc(sem("router_in"), 16)
            pool.dma_start(r_e, a["router_expert_w"][l].rearrange("(p t) n -> p t n", t=KT)).then_inc(sem("router_in"), 16)
            pool.dma_start(r_b[:, 0:NG], a["router_group_b"][l:l + 1, :].to_broadcast((P, NG))).then_inc(sem("router_in"), 16)
            pool.dma_start(r_b[:, NG:NG + NX], a["router_expert_b"][l:l + 1].rearrange("a g e -> a (g e)")
                           .to_broadcast((P, NX))).then_inc(sem("router_in"), 16)
            with pool.Fori(0, NG) as g:
                for u in range(NE):
                    store_unit(u, g, NX * (l + 1) + g * NE + u + 1, first_dst(1, u, g) if l == 0 else second_dst(u, g),
                               1 if l == 0 else 2)
        pool.wait_ge(sem("h_done"), 4)
        row_load(3, a["final_norm_g"].rearrange("(a n) -> a n", a=1).to_broadcast((P, D)))
        for par in range(2):
            pool.wait_ge(sem(f"ada_out{par}"), 16 * (16 + 16 + 32))
        if TWO:
            pool_second(pool)

    def stick_act(act, link, copy):
        for k in range(HEADS_S + 2):
            if k < HEADS_S:
                act.wait_ge(sem("s_z"), k + 1)
                t, e_ = sb_t[:, k % 2, :], sb_e[:, k % 2, :]
                if k >= 2:
                    act.wait_ge(sem("s_sp"), k - 1)
                link(nc.scalar.activation(t, bank[k % 3][:, 0:384], ACT.Abs))
                link(nc.scalar.activation(t, t, ACT.Exp, scale=-1.0))
                nc.scalar.activation(e_, t, ACT.Ln, bias=1.0).then_inc(sem("s_ln"), 1)
            if 1 <= k <= HEADS_S:
                j = k - 1
                act.wait_ge(sem("s_log"), j + 1)
                nc.scalar.activation(sb_a[:, j % 2, :], sb_a[:, j % 2, :], ACT.Exp).then_inc(sem("s_a"), 1)
            if k >= 2 and k % 2 == 1:
                c = (k - 3) // 2
                act.wait_ge(sem("s_pv"), 2 * c + 2)
                copy(oT[:, c, :], bank[3 + c % 2][:, 0:S]).then_inc(sem("oT"), 1)

    @block.scalar
    def _(act):
        link = Chain(act, sem("act_step"))
        copy = lambda o_, i_: nc.scalar.activation(o_, i_, ACT.Copy)

        def square_norm(n):
            if n:
                act.wait_ge(sem("x_done"), n)
            else:
                act.wait_ge(sem("x_in"), 16)
            for t in range(TT):
                link(nc.scalar.activation(h[:, t, :], x[:, t, :], ACT.Square, accum_out=ss[:, t:t + 1]))
            act.wait_ge(sem("eps"), 1)
            nc.scalar.activation(ss, ss, ACT.Sqrt, scale=1.0 / D, bias=small[:, 40:41]).then_inc(sem("rms"), 1)

        def take_hT(n):
            for j in range(4):
                act.wait_ge(sem("hT_mm"), 4 * n + j + 1)
                copy(hT[:, 2 * j:2 * j + 2, :], bank[j][:].rearrange("p (t s) -> p t s", t=2)).then_inc(sem("hT_done"), 1)

        def take_qkv(l):
            for i in range(12):
                act.wait_ge(sem("qkv_mm"), EACH["qkv_mm"] * l + i + 1)
                src = bank[i % 4][:]
                if i < 8:
                    dst = (qT, kT)[i // 4][:, 2 * (i % 4):2 * (i % 4) + 2, :]
                    ins = nc.scalar.activation(dst, src.rearrange("p (c s) -> p c s", c=2), ACT.Copy,
                                               scale=HD ** -0.5 if i < 4 else 1.0)
                else:
                    ins = copy(v[:, (i - 8) // 2, (i % 2) * 512:(i % 2 + 1) * 512], src)
                ins.then_inc(sem("qkv"), 1)

        def diff_exp(u):
            nk = P if u % 2 == 0 else S
            act.wait_ge(sem("d_scores"), u + 1)
            for m in range(2):
                nc.scalar.activation(pr[:, u % 2, m, 0:nk], sc_[:, u % 2, m, 0:nk], ACT.Exp,
                                     bias=small[:, 48 + 2 * (u % 2) + m:49 + 2 * (u % 2) + m],
                                     accum_out=small[:, 56 + 2 * (u % 2) + m:57 + 2 * (u % 2) + m]).then_inc(sem("d_exp"), 1)

        def diff_awT(u):
            n = 1 + u % 2
            act.wait_ge(sem("d_tr"), u + 1)
            copy(awT[:, u % 2, 0:n, :], bank[6][:, 0:n * P].rearrange("p (k q) -> p k q", k=n)).then_inc(sem("d_awT"), 1)

        def take_oT(l):
            for j in range(4):
                act.wait_ge(sem("oT_mm"), j + 1)
                copy(oT[:, 2 * j:2 * j + 2, :], bank[j][:].rearrange("p (t s) -> p t s", t=2)).then_inc(sem("oT"), 1)

        def experts(l):
            mb = M_BASE[l]
            act.wait_ge(sem("hover_mm"), EACH["hover_mm"] * l + 1)
            for k in range(2):
                copy(hover[:, 4 * k:4 * k + 4, :], bank[4 + 3 * k][:].rearrange("p (t s) -> p t s", t=4)).then_inc(
                    sem("hover"), 1)
            act.wait_ge(sem("wsl_mm"), EACH["wsl_mm"] * l + 1)
            copy(wsl, bank[5][:, 0:2 * NX]).then_inc(sem("wsl"), 1)
            act.wait_ge(sem("cnt"), EACH["cnt"] * l + 1)
            with act.Fori(0, NG) as g:
                n_g = act.value_load(cnt[0:1, bass.ds(g, 1)], min_val=0, max_val=S)
                act.wait_ge(sem("gather_mm"), EACH["gather_mm"] * l + g + 1)
                for k in range(2):
                    copy(hcur[:, 4 * k:4 * k + 4, :], bank[4 + 3 * k][:].rearrange("p (t s) -> p t s", t=4)).then_inc(
                        sem("hcur"), 1)

                def silu(e):
                    act.wait_ge(sem("gu"), EACH["gu"] * l + g * NE + e + 1)
                    nc.scalar.activation(s_act, bank[2 * (e % 2)][:], ACT.Silu).then_inc(sem("silu"), 1)

                def take_hid(e):
                    act.wait_ge(sem("hid_tr"), EACH["hid_tr"] * l + g * NE + e + 1)
                    copy(hidT, bank[4][:].rearrange("p (t s) -> p t s", t=FK)).then_inc(sem("hidT"), 1)

                for e in range(NE):
                    if e:
                        take_hid(e - 1)
                    silu(e)
                    with act.If(n_g > P):
                        act.wait_ge(sem(f"o_gu{l}"), e + 1)
                        act.wait_ge(sem("hid"), EACH["hid"] * l + g * NE + e + 1)
                        nc.scalar.activation(s_act, bank[2 * ((e + 1) % 2)][:], ACT.Silu).then_inc(sem(f"o_silu{l}"), 1)
                        act.wait_ge(sem(f"o_tr{l}"), e + 1)
                        copy(hidT, bank[4][:].rearrange("p (t s) -> p t s", t=FK)).then_inc(sem(f"o_hidT{l}"), 1)
                take_hid(NE - 1)
                act.wait_ge(sem("group_mm"), EACH["group_mm"] * l + g + 1)
                for k in range(2):
                    copy(acc[:, bass.ds(g, 1), 512 * k:512 * k + 512].rearrange("p g n -> p (g n)"),
                         bank[5 + k][:]).then_inc(sem("acc"), 1)
            for k in range(3):
                act.wait_ge(sem("selT_mm"), EACH["selT_mm"] * l + k + 1)
                w = min(512, (NG + 1) * S - 512 * k)
                flat = selT.rearrange("p g s -> p (g s)")
                copy(flat[:, 512 * k:512 * k + w], bank[5 + k][:, 0:w]).then_inc(sem("selT"), 1)

        act.wait_ge(sem("cond_in"), 48)
        nc.scalar.activation(cond, cond, ACT.Silu).then_inc(sem("cond"), 1)
        for l in range(2):
            square_norm(2 * l)
            take_hT(2 * l)
            take_qkv(l)
            if l == 0:
                act.wait_ge(sem("lam_dot"), 1)
                nc.scalar.activation(lvec[:, 2:4], lvec[:, 0:2], ACT.Exp).then_inc(sem("lam_exp"), 1)
                for k in range(16 + 2):
                    if k >= 2:
                        diff_awT(k - 2)
                    if k < 16:
                        diff_exp(k)
                act.wait_ge(sem("sub_ss"), 1)
                nc.scalar.activation(small[:, 80:96], small[:, 64:80], ACT.Sqrt, scale=1.0 / P,
                                     bias=small[:, 41:42]).then_inc(sem("sub_rms"), 1)
                take_oT(l)
            else:
                stick_act(act, link, copy)
            square_norm(2 * l + 1)
            take_hT(2 * l + 1)
            act.wait_ge(sem("gdiff"), EACH["gdiff"] * l + 1)
            nc.scalar.activation(eg, g4c, ACT.Exp).then_inc(sem("r_exp"), 1)
            act.wait_ge(sem("ediff"), EACH["ediff"] * l + 1)
            nc.scalar.activation(ex, den, ACT.Exp).then_inc(sem("r_exp"), 1)
            experts(l)
        square_norm(4)
        if TWO:
            act_second(act, link, copy)

    @block.vector
    def _(dve):
        link = Chain(dve, sem("dve_step"))
        V = nc.vector

        def ada_math(u, n, conds, part=0):
            nconds = len(conds)
            dve.wait_ge(sem(f"ada_in{u % 2}"), 32 * ADA_IN(n, u))
            for k, c in enumerate(conds):
                w = ada_w[:, u % 2, :].rearrange("p (t n) -> p t n", t=KT)
                prod = ada_prod.rearrange("p (t n) -> p t n", t=KT)
                ins = V.tensor_tensor(prod, w, cond[:, c, :].unsqueeze(2).to_broadcast((P, KT, UC)), ALU.mult)
                ins.then_inc(sem("ada_mul"), 1)
                dve.wait_ge(sem("ada_mul"), MUL(n) + k + 1)
                ins = V.tensor_reduce(ada_acc[:, u % 2, k * UC:(k + 1) * UC], ada_prod.rearrange("p (t n) -> p n t", t=KT),
                                      AX.X, ALU.add)
                ins.then_inc(sem("ada_sum"), 1)
                dve.wait_ge(sem("ada_sum"), MUL(n) + k + 1)

        def ada_take(u, n, nconds):
            dve.wait_ge(sem("ada_mm"), n + 1)
            if not isinstance(n, int) or n >= 2:
                dve.wait_ge(sem(f"ada_out{u % 2}"), 16 * OUTS(n, u))
            for k in range(nconds):
                ins = V.tensor_tensor(ada_row[0:1, u % 2, k * UC:(k + 1) * UC], bank[7][0:1, k * UC:(k + 1) * UC],
                                      ada_bias[0:1, u % 2, :], ALU.add)
                if k < nconds - 1:
                    ins.then_inc(sem("ada_half"), 1)
            ins.then_inc(sem("ada_row"), 1)

        ada_base = [0]
        ADA_IN = lambda n, u: n_half(n, u) + 1
        n_half = lambda n, u: HALF[0]
        HALF = [0]
        MULV, OUTV = [0], [0]
        MUL = lambda n: MULV[0]
        OUTS = lambda n, u: OUTV[0]

        def set_counts(l, g, u):
            HALF[0] = 16 * l + g * 4 + u // 2
            per = 2 if l == 2 else 1
            MULV[0] = (0 if l == 0 else 32 if l == 1 else 64) + (g * 8 + u) * per
            OUTV[0] = (0 if l == 0 else 16 if l == 1 else 32) + (g * 4 + u // 2) * per

        conds_of = lambda l: [0] if l < 2 else [1, 2]

        def norm_rows(n):
            dve.wait_ge(sem("rows_in"), 64 * (n + 1))
            link(V.scalar_tensor_tensor(rows[:, 0, :], rows[:, 0, :], 1.0, rows[:, 3, :], ALU.add, ALU.mult))
            dve.wait_ge(sem("rms"), n + 1)
            link(V.reciprocal(rstd, ss))
            for t in range(TT):
                link(V.scalar_tensor_tensor(h[:, t, :], x[:, t, :], rstd[:, t:t + 1], rows[:, 0, :], ALU.mult, ALU.mult))
            link(V.tensor_tensor(h[:, 0, :], h[:, 0, :], rows[:, 1, :], ALU.add))
            V.tensor_tensor(h[:, 1, :], h[:, 1, :], rows[:, 1, :], ALU.add).then_inc(sem("h_done"), 1)
            dve.wait_ge(sem("h_done"), n + 1)

        def update_x(n, name, scr):
            gate = rows[:, 2 if n % 2 == 0 else 4, :]
            for i in range(4):
                t, hf = i // 2, i % 2
                dve.wait_ge(sem(name), EACH[name] * (n // 2) + i + 1)
                link(V.tensor_tensor(scr[:, t, hf * 512:hf * 512 + 512], bank[i][:], gate[:, hf * 512:hf * 512 + 512], ALU.mult))
            link(V.tensor_tensor(x[:, 0, :], x[:, 0, :], scr[:, 0, :], ALU.add))
            V.tensor_tensor(x[:, 1, :], x[:, 1, :], scr[:, 1, :], ALU.add).then_inc(sem("x_done"), 1)
            dve.wait_ge(sem("x_done"), n + 1)

        def diff_scores(u):
            hd, qt = u // 2, u % 2
            nk = S if qt else P
            dve.wait_ge(sem("d_s"), u + 1)
            if u >= 2:
                dve.wait_ge(sem("d_exp"), 2 * (u - 1))
            s3 = psum[:, 2 * (u % 2):2 * (u % 2) + 2, 0:nk]
            dist = C["dist1" if qt else "dist0"].unsqueeze(1).to_broadcast((P, 2, nk))
            link(V.scalar_tensor_tensor(sc_[:, u % 2, :, 0:nk], dist, 2.0 ** (-(hd + 1)), s3, ALU.mult, ALU.add))
            V.tensor_reduce(small[:, 48 + 2 * (u % 2):50 + 2 * (u % 2)], sc_[:, u % 2, :, 0:nk], AX.X, ALU.max,
                            negate=True).then_inc(sem("d_scores"), 1)
            dve.wait_ge(sem("d_scores"), u + 1)

        def diff_combine(u):
            nk = S if u % 2 else P
            dve.wait_ge(sem("d_exp"), 2 * u + 2)
            if u >= 2:
                dve.wait_ge(sem("d_tr"), u - 1)
            r = small[:, 60 + 2 * (u % 2):62 + 2 * (u % 2)]
            sums = small[:, 56 + 2 * (u % 2):58 + 2 * (u % 2)]
            link(V.reciprocal(r, sums))
            link(V.tensor_scalar(r[:, 1:2], r[:, 1:2], lam, None, ALU.mult))
            link(V.tensor_scalar(aw[:, u % 2, 0:nk], pr[:, u % 2, 1, 0:nk], r[:, 1:2], None, ALU.mult))
            V.scalar_tensor_tensor(aw[:, u % 2, 0:nk], pr[:, u % 2, 0, 0:nk], r[:, 0:1], aw[:, u % 2, 0:nk],
                                   ALU.mult, ALU.add).then_inc(sem("d_a"), 1)
            dve.wait_ge(sem("d_a"), u + 1)

        def diff_out(u):
            dve.wait_ge(sem("d_pv"), u + 1)
            V.tensor_copy(o[:, u % 2, (u // 2) * P:(u // 2 + 1) * P], bank[4 + u % 2][:, 0:P]).then_inc(sem("d_o"), 1)

        def router(l):
            bc = lambda t, n_: t.unsqueeze(2).to_broadcast((P, TT, n_))
            dve.wait_ge(sem("router_in"), 64 * (l + 1))
            dve.wait_ge(sem("logits"), EACH["logits"] * l + 1)
            lg = bank[0][:, 0:TT * NG].rearrange("p (t n) -> p t n", t=TT)
            le = bank[1][:, 0:TT * NX].rearrange("p (t n) -> p t n", t=TT)
            link(V.tensor_tensor(g4, lg, r_b[:, 0:NG].unsqueeze(1).to_broadcast((P, TT, NG)), ALU.add))
            link(V.tensor_tensor(e32, le, r_b[:, NG:].unsqueeze(1).to_broadcast((P, TT, NX)), ALU.add))

            def first_max(hot, t_, mx, tmp, prio, n_):
                link(V.tensor_reduce(mx, t_, AX.X, ALU.max))
                link(V.tensor_tensor(tmp, t_, bc(mx, n_), ALU.is_ge))
                link(V.tensor_tensor(tmp, tmp, prio.unsqueeze(1).to_broadcast((P, TT, n_)), ALU.mult))
                link(V.tensor_reduce(pm, tmp, AX.X, ALU.max))
                link(V.tensor_tensor(hot, tmp, bc(pm, n_), ALU.is_equal))

            first_max(og, g4, gm, g4b, C["prio4"], NG)
            V.tensor_tensor(g4c, g4, bc(gm, NG), ALU.subtract).then_inc(sem("gdiff"), 1)
            e4 = e32.rearrange("p t (g e) -> p t g e", g=NG)
            e4b = e32b.rearrange("p t (g e) -> p t g e", g=NG)
            for t in range(TT):
                link(V.tensor_tensor(e4b[:, t], e4[:, t], og[:, t].unsqueeze(2).to_broadcast((P, NG, NE)), ALU.mult))
            link(V.tensor_reduce(e8, e32b.rearrange("p t (g e) -> p t e g", g=NG), AX.X, ALU.add))
            first_max(o1, e8, m1, t8, C["prio8"], NE)
            link(V.scalar_tensor_tensor(e8b, o1, -3e38, e8, ALU.mult, ALU.add))
            first_max(o2, e8b, m2, t8, C["prio8"], NE)
            V.tensor_tensor(den, m2, m1, ALU.subtract).then_inc(sem("ediff"), 1)
            dve.wait_ge(sem("r_exp"), EACH["r_exp"] * l + 2)
            link(V.tensor_reduce(gs, eg, AX.X, ALU.add))
            link(V.tensor_scalar(den, ex, 1.0, None, ALU.add))
            link(V.tensor_tensor(den, den, gs, ALU.mult))
            link(V.reciprocal(w1, den))
            link(V.tensor_tensor(w2, w1, ex, ALU.mult))
            link(V.tensor_tensor(t8, o1, bc(w1, NE), ALU.mult))
            link(V.tensor_tensor(e8b, o2, bc(w2, NE), ALU.mult))
            link(V.tensor_tensor(t8, t8, e8b, ALU.add))
            w4 = w32.rearrange("p t (g e) -> p t g e", g=NG)
            for t in range(TT):
                link(V.tensor_tensor(w4[:, t], t8[:, t].unsqueeze(1).to_broadcast((P, NG, NE)),
                                     og[:, t].unsqueeze(2).to_broadcast((P, NG, NE)), ALU.mult))
            V.tensor_tensor(ogs, og[:, 0], og[:, 1], ALU.add).then_inc(sem("og"), 1)
            dve.wait_ge(sem("rank_mm"), EACH["rank_mm"] * l + 1)
            rank = bank[2][:, 0:TT * NG].rearrange("p (t g) -> p t g", t=TT)
            link(V.tensor_tensor(rkt, rank, og, ALU.mult))
            link(V.tensor_reduce(rk, rkt, AX.X, ALU.add))
            V.tensor_copy(cnt[0:1, 0:NG], bank[2][0:1, TT * NG:TT * NG + NG]).then_inc(sem("cnt"), 1)
            for t in range(TT):
                for g in range(NG):
                    link(V.tensor_scalar(sel[:, t, g, :], C["iota"], rk[:, t:t + 1], og[:, t, g:g + 1], ALU.is_equal, ALU.mult))
                ins = V.tensor_scalar(sel[:, t, NG, :], C["iota_over"], rk[:, t:t + 1], None, ALU.is_equal)
                ins.then_inc(sem("sel"), 1)
            dve.wait_ge(sem("sel"), EACH["sel"] * l + TT)

        def experts(l):
            dve.wait_ge(sem("wsl"), EACH["wsl"] * l + 1)
            V.memset(acc[:, NG, :], 0.0).then_inc(sem("over_zero"), 1)
            dve.wait_ge(sem("over_zero"), EACH["over_zero"] * l + 1)
            dve.wait_ge(sem("cnt"), EACH["cnt"] * l + 1)
            conds = conds_of(l + 1)
            with dve.Fori(0, NG) as g:
                n_g = dve.value_load(cnt[0:1, bass.ds(g, 1)], min_val=0, max_val=S)
                for e in range(NE):
                    set_counts(l + 1, g, e)
                    n = NX * (l + 1) + g * NE + e
                    ada_math(e, n, conds)
                    ada_take(e, n, len(conds))
                    dve.wait_ge(sem("silu"), EACH["silu"] * l + g * NE + e + 1)
                    V.scalar_tensor_tensor(hid, s_act, wsl[:, bass.ds(g * NE + e, 1)], bank[2 * (e % 2) + 1][:],
                                           ALU.mult, ALU.mult).then_inc(sem("hid"), 1)
                    with dve.If(n_g > P):
                        dve.wait_ge(sem(f"o_silu{l}"), e + 1)
                        V.scalar_tensor_tensor(s_act, s_act, wsl[:, bass.ds(g * NE + e + NX, 1)],
                                               bank[2 * ((e + 1) % 2) + 1][:], ALU.mult, ALU.mult).then_inc(sem(f"o_hid{l}"), 1)
                        dve.wait_ge(sem(f"o_down{l}"), e + 1)
                        for k in range(2):
                            V.tensor_tensor(acc[:, NG, 512 * k:512 * k + 512], acc[:, NG, 512 * k:512 * k + 512],
                                            bank[2 * ((e + 1) % 2) + k][:], ALU.add).then_inc(sem(f"o_add{l}"), 1)
                        dve.wait_ge(sem(f"o_add{l}"), 2 * e + 2)

        V.memset(small[:, 40:41], 1e-6).then_inc(sem("eps0"), 1)
        dve.wait_ge(sem("eps0"), 1)
        V.memset(small[:, 41:42], 1e-5).then_inc(sem("eps"), 1)
        dve.wait_ge(sem("consts"), 16)
        dve.wait_ge(sem("cond"), 1)
        for g in range(NG):
            for u in range(NE):
                set_counts(0, g, u)
                ada_math(u, g * NE + u, [0])
                ada_take(u, g * NE + u, 1)
        for l in range(2):
            norm_rows(2 * l)
            if l == 0:
                dve.wait_ge(sem("lam_in"), 16 * 5)
                link(V.tensor_tensor(lqk[:, 0:4:2, :], lqk[:, 0:4:2, :], lqk[:, 1:4:2, :], ALU.mult))
                V.tensor_reduce(lvec[:, 0:2], lqk[:, 0:4:2, :], AX.X, ALU.add).then_inc(sem("lam_dot"), 1)
                dve.wait_ge(sem("lam_exp"), 1)
                link(V.tensor_tensor(lam, lvec[:, 3:4], lvec[:, 2:3], ALU.subtract))
                link(V.tensor_scalar(lam, lam, -0.2, None, ALU.add))
                for k in range(16 + 3):
                    if k < 16:
                        diff_scores(k)
                    if 1 <= k <= 16:
                        diff_combine(k - 1)
                    if k >= 3:
                        diff_out(k - 3)
                dve.wait_ge(sem("d_o"), 16)
                o4 = o.rearrange("p t (h e) -> p (t h) e", h=HEADS_D)
                sq = qT.rearrange("p a b -> p (a b)").rearrange("p (g e) -> p g e", e=P)
                link(V.tensor_tensor(sq, o4, o4, ALU.mult))
                V.tensor_reduce(small[:, 64:80], sq, AX.X, ALU.add).then_inc(sem("sub_ss"), 1)
                dve.wait_ge(sem("sub_rms"), 1)
                link(V.reciprocal(small[:, 80:96], small[:, 80:96]))
                link(V.tensor_scalar(sub_g, sub_g, 0.8, None, ALU.mult))
                link(V.tensor_tensor(o4, o4, small[:, 80:96].unsqueeze(2).to_broadcast((P, 16, P)), ALU.mult))
                V.tensor_tensor(o4, o4, sub_g.unsqueeze(1).to_broadcast((P, 16, P)), ALU.mult).then_inc(sem("sub_done"), 1)
                dve.wait_ge(sem("sub_done"), 1)
            else:
                link(V.tensor_scalar(hide, C["strict"], 1.0, -NBIG, ALU.subtract, ALU.mult))
                for k in range(HEADS_S + 1):
                    if k < HEADS_S:
                        dve.wait_ge(sem("s_ln"), k + 1)
                        if k >= 2:
                            dve.wait_ge(sem("s_c"), k - 1)
                        link(V.scalar_tensor_tensor(sb_sp[:, k % 2, :], bank[k % 3][:, 0:384], 0.0, sb_e[:, k % 2, :],
                                                    ALU.max, ALU.add))
                        V.tensor_tensor(sb_sp[:, k % 2, :], sb_sp[:, k % 2, :], C["strict"], ALU.mult).then_inc(sem("s_sp"), 1)
                    if k >= 1:
                        j = k - 1
                        dve.wait_ge(sem("s_c"), j + 1)
                        if j >= 2:
                            dve.wait_ge(sem("s_pv"), j - 1)
                        V.scalar_tensor_tensor(sb_a[:, j % 2, :], bank[j % 3][:, 0:384], 0.0, hide,
                                               ALU.min, ALU.add).then_inc(sem("s_log"), 1)
            update_x(2 * l, "proj_mm", v)
            norm_rows(2 * l + 1)
            if dbg: dve.wait_ge(sem("dbg"), 16*l+16)
            router(l)
            experts(l)
            update_x(2 * l + 1, "y_mm", h)
        dve.wait_ge(sem("rows_in"), 16 * 17)
        dve.wait_ge(sem("rms"), 5)
        link(V.reciprocal(rstd, ss))
        link(V.scalar_tensor_tensor(x[:, 0, :], x[:, 0, :], rstd[:, 0:1], rows[:, 3, :], ALU.mult, ALU.mult))
        V.scalar_tensor_tensor(x[:, 1, :], x[:, 1, :], rstd[:, 1:2], rows[:, 3, :], ALU.mult, ALU.mult).then_inc(sem("final"), 1)
        dve.wait_ge(sem("final"), 1)
        if TWO:
            dve_second(dve, link)

    @block.tensor
    def _(pe):
        T = nc.tensor

        def mm(out_, lhsT, rhs, start, stop):
            return T.matmul(out_, lhsT, rhs, start=start, stop=stop, skip_group_check=True)

        def ada_mm(u, n, nconds):
            pe.wait_ge(sem("ada_sum"), SUM(n))
            mm(bank[7][0:1, 0:nconds * UC], C["ones"][:, 0:1], ada_acc[:, u % 2, 0:nconds * UC], True, True).then_inc(
                sem("ada_mm"), 1)

        def transpose_h(n):
            pe.wait_ge(sem("h_done"), n + 1)
            for j in range(4):
                for i in range(4):
                    t, tile = 2 * j + i // 2, i % 2
                    ins = T.transpose(bank[j][:, i * P:(i + 1) * P], h[:, tile, t:D:KT], ident)
                ins.then_inc(sem("hT_mm"), 1)

        def qkv(l):
            b = L_BASE[l]
            pe.wait_ge(sem("hT_done"), 8 * l + 4)
            for i in range(12):
                n = b + (i // 2 if i < 8 else 4 + i % 2)
                if i < 10:
                    loaded(pe, n)
                if i >= 4:
                    pe.wait_ge(sem("qkv"), EACH["qkv"] * l + i - 3)
                w = wslot(n, KT, 512)
                if i < 8:
                    for c in range(2):
                        for t in range(KT):
                            col = (i % 2) * 256 + c * P
                            ins = mm(bank[i % 4][:, c * S:(c + 1) * S], w[:, t, col:col + P], hT[:, t, :], t == 0, t == KT - 1)
                    if i % 2:
                        ins.then_inc(free(n), 1)
                        pe.wait_ge(free(n), n // RING + 1)
                        pe.sem_inc(sem("qkv_mm"), 1)
                    else:
                        ins.then_inc(sem("qkv_mm"), 1)
                else:
                    tile = (i - 8) // 2
                    for t in range(KT):
                        ins = mm(bank[i % 4][:], hT[:, t, tile * P:(tile + 1) * P], w[:, t, :], t == 0, t == KT - 1)
                    if tile:
                        ins.then_inc(free(n), 1)
                        pe.wait_ge(free(n), n // RING + 1)
                        pe.sem_inc(sem("qkv_mm"), 1)
                    else:
                        ins.then_inc(sem("qkv_mm"), 1)

        def projection(l):
            b = L_BASE[l]
            for hf in range(2):
                loaded(pe, b + 6 + hf)
            for i in range(4):
                tile, hf = i // 2, i % 2
                w = wslot(b + 6 + hf, KT, 512)
                for t in range(KT):
                    ins = mm(bank[i][:], oT[:, t, tile * P:(tile + 1) * P], w[:, t, :], t == 0, t == KT - 1)
                ins.then_inc(sem("proj_mm"), 1)
            for hf in range(2):
                pe.wait_ge(sem("proj_mm"), EACH["proj_mm"] * l + 4)
                pe.sem_inc(free(b + 6 + hf), 1)

        def diff_attention():
            pe.wait_ge(sem("qkv"), 12)
            for k in range(16 + 3):
                if k < 16:
                    hd, qt = k // 2, k % 2
                    nk = S if qt else P
                    if k >= 2:
                        pe.wait_ge(sem("d_scores"), k - 1)
                    for m in range(2):
                        lo = m * HD
                        ins = mm(bank[2 * (k % 2) + m][:, 0:nk], qT[lo:lo + HD, hd, qt * P:(qt + 1) * P],
                                 kT[lo:lo + HD, hd, 0:nk], True, True)
                    ins.then_inc(sem("d_s"), 1)
                if 2 <= k < 18:
                    u = k - 2
                    pe.wait_ge(sem("d_a"), u + 1)
                    if u:
                        pe.wait_ge(sem("d_awT"), u)
                    for j in range(1 + u % 2):
                        ins = T.transpose(bank[6][:, j * P:(j + 1) * P], aw[:, u % 2, j * P:(j + 1) * P], ident)
                    ins.then_inc(sem("d_tr"), 1)
                if k >= 3:
                    u = k - 3
                    hd = u // 2
                    pe.wait_ge(sem("d_awT"), u + 1)
                    if u >= 2:
                        pe.wait_ge(sem("d_o"), u - 1)
                    n = 1 + u % 2
                    for j in range(n):
                        ins = mm(bank[4 + u % 2][:, 0:P], awT[:, u % 2, j, :], v[:, j, hd * P:(hd + 1) * P],
                                 j == 0, j == n - 1)
                    ins.then_inc(sem("d_pv"), 1)
            pe.wait_ge(sem("sub_done"), 1)
            for j in range(4):
                for i in range(4):
                    t, tile = 2 * j + i // 2, i % 2
                    ins = T.transpose(bank[j][:, i * P:(i + 1) * P], o[:, tile, t * P:(t + 1) * P], ident)
                ins.then_inc(sem("oT_mm"), 1)
            pe.wait_ge(sem("oT"), 4)

        def stick_attention():
            pe.wait_ge(sem("qkv"), 24)
            for k in range(HEADS_S + 2):
                if k < HEADS_S:
                    c, lo = k // 2, HD * (k % 2)
                    if k >= 3:
                        pe.wait_ge(sem("s_log"), k - 2)
                    b = bank[k % 3]
                    mm(b[:, 0:S], kT[lo:lo + HD, c, 0:P], qT[lo:lo + HD, c, :], True, True)
                    mm(b[:, S:384], kT[lo:lo + HD, c, P:S], qT[lo:lo + HD, c, P:S], False, True).then_inc(sem("s_z"), 1)
                if 1 <= k <= HEADS_S:
                    j = k - 1
                    b, s = bank[j % 3], sb_sp[:, j % 2, :]
                    pe.wait_ge(sem("s_sp"), j + 1)
                    mm(b[:, 0:S], C["suffix"], s[:, 0:S], False, True)
                    mm(b[:, P:S], C["minus"], s[:, S:384], False, True)
                    mm(b[:, S:384], C["suffix"], s[:, S:384], False, True).then_inc(sem("s_c"), 1)
                if k >= 2:
                    j = k - 2
                    c, lo = j // 2, HD * (j % 2)
                    b = bank[3 + c % 2]
                    pe.wait_ge(sem("s_a"), j + 1)
                    if c >= 2:
                        pe.wait_ge(sem("oT"), 4 + c - 1)
                    hd = slice(j * HD, (j + 1) * HD)
                    mm(b[lo:lo + HD, 0:S], v[:, 0, hd], sb_a[:, j % 2, 0:S], True, False)
                    mm(b[lo:lo + HD, P:S], v[:, 1, hd], sb_a[:, j % 2, S:384], False, True).then_inc(sem("s_pv"), 1)
            pe.wait_ge(sem("oT"), 12)

        def router(l):
            pe.wait_ge(sem("hT_done"), 8 * l + 8)
            pe.wait_ge(sem("router_in"), 64 * (l + 1))
            for tile in range(TT):
                for t in range(KT):
                    lhs = hT[:, t, tile * P:(tile + 1) * P]
                    mm(bank[0][:, tile * NG:(tile + 1) * NG], lhs, r_g[:, t, :], t == 0, t == KT - 1)
                    ins = mm(bank[1][:, tile * NX:(tile + 1) * NX], lhs, r_e[:, t, :], t == 0, t == KT - 1)
            ins.then_inc(sem("logits"), 1)
            pe.wait_ge(sem("og"), EACH["og"] * l + 1)
            r = bank[2]
            mm(r[:, 0:NG], C["before"], og[:, 0], True, True)
            mm(r[:, NG:2 * NG], C["ones"], og[:, 0], True, False)
            mm(r[:, NG:2 * NG], C["before"], og[:, 1], False, True)
            mm(r[:, 2 * NG:3 * NG], C["ones"], ogs, True, True).then_inc(sem("rank_mm"), 1)
            pe.wait_ge(sem("sel"), EACH["sel"] * l + TT)
            gather(sel[:, :, NG, :]).then_inc(sem("hover_mm"), 1)
            for g in range(NG):
                for tile in range(TT):
                    mm(bank[5][:, g * NE:(g + 1) * NE], sel[:, tile, g, :], w32[:, tile, g * NE:(g + 1) * NE], tile == 0, tile == 1)
            for tile in range(TT):
                ins = mm(bank[5][:, NX:2 * NX], sel[:, tile, NG, :], w32[:, tile, :], tile == 0, tile == 1)
            ins.then_inc(sem("wsl_mm"), 1)
            pe.wait_ge(sem("hover"), EACH["hover"] * l + 2)
            pe.wait_ge(sem("wsl"), EACH["wsl"] * l + 1)

        def gather(pick):
            for t in range(KT):
                for tile in range(TT):
                    ins = mm(bank[4 + 3 * (t // 4)][:, (t % 4) * P:(t % 4 + 1) * P], h[:, tile, t:D:KT], pick[:, tile],
                             tile == 0, tile == 1)
            return ins

        def experts(l):
            mb = M_BASE[l]
            nconds = l + 1
            pe.wait_ge(sem("cnt"), EACH["cnt"] * l + 1)
            with pe.Fori(0, NG) as g:
                n_g = pe.value_load(cnt[0:1, bass.ds(g, 1)], min_val=0, max_val=S)
                pe.wait_ge(sem("ada_row"), NX * (l + 1) + g * NE)
                gather(sel[:, :, bass.ds(g, 1), :].rearrange("p t g s -> p t (g s)")).then_inc(sem("gather_mm"), 1)
                pe.wait_ge(sem("hcur"), EACH["hcur"] * l + 2 * g + 2)

                def gate_up(e, j, t0, t1, who, b):
                    w = wslot(mb + 3 * e + j, KT, 512)
                    for t in range(t0, t1):
                        ins = mm(bank[b + j][:], who[:, t, :], w[:, t, :], t == 0, t == KT - 1)
                    return ins

                def turn(src, b_sem):
                    for t in range(FK):
                        ins = T.transpose(bank[4][:, t * P:(t + 1) * P], src[:, t:FH:FK], ident)
                    ins.then_inc(b_sem, 1)

                def down(e, b0, first, last_):
                    w = ring[:, slot(mb + 3 * e + 2), :].rearrange("p (t n) -> p t n", t=FK)
                    for t in range(FK):
                        for k in range(2):
                            ins = mm(bank[b0 + k][:], hidT[:, t, :], w[:, t, k * 512:(k + 1) * 512], first and t == 0, last_ and t == FK - 1)
                    return ins

                for e in range(NE + 1):
                    b = 2 * (e % 2)
                    if e < NE:
                        loaded(pe, mb + 3 * e, g)
                        gate_up(e, 0, 0, KT, hcur, b)
                    if e:
                        pe.wait_ge(sem("hid"), EACH["hid"] * l + g * NE + e)
                        turn(hid, sem("hid_tr"))
                    if e < NE:
                        loaded(pe, mb + 3 * e + 1, g)
                        gate_up(e, 1, 0, KT - 1, hcur, b)
                    if e < NE:
                        pe.wait_ge(sem("ada_sum"), (32 if l == 0 else 64) + (g * NE + e + 1) * nconds)
                        mm(bank[7][0:1, 0:nconds * UC], C["ones"][:, 0:1], ada_acc[:, e % 2, 0:nconds * UC], True, True).then_inc(
                            sem("ada_mm"), 1)
                    if e:
                        loaded(pe, mb + 3 * (e - 1) + 2, g)
                        pe.wait_ge(sem("hidT"), EACH["hidT"] * l + g * NE + e)
                        down(e - 1, 5, e == 1, e == NE).then_inc(free(mb + 3 * (e - 1) + 2), 1)
                    if e < NE:
                        gate_up(e, 1, KT - 1, KT, hcur, b).then_inc(sem("gu"), 1)
                        with pe.If(n_g > P):
                            ob = 2 * ((e + 1) % 2)
                            gate_up(e, 0, 0, KT, hover, ob).then_inc(free(mb + 3 * e), 1)
                            gate_up(e, 1, 0, KT, hover, ob).then_inc(free(mb + 3 * e + 1), 1)
                            pe.wait_ge(free(mb + 3 * e + 1), (mb + 3 * e + 1) // RING + 1 + 4 * g)
                            pe.sem_inc(sem(f"o_gu{l}"), 1)
                            pe.wait_ge(sem(f"o_hid{l}"), e + 1)
                            turn(s_act, sem(f"o_tr{l}"))
                            loaded(pe, mb + 3 * e + 2, g)
                            pe.wait_ge(sem(f"o_hidT{l}"), e + 1)
                            down(e, ob, True, True).then_inc(sem(f"o_down{l}"), 1)
                            pe.wait_ge(sem(f"o_add{l}"), 2 * e + 2)
                        with pe.Else():
                            pe.wait_ge(sem("gu"), EACH["gu"] * l + g * NE + e + 1)
                            pe.sem_inc(free(mb + 3 * e), 1)
                            pe.sem_inc(free(mb + 3 * e + 1), 1)
                pe.wait_ge(free(mb + 3 * NE - 1), (mb + 3 * NE - 1) // RING + 1 + 4 * g)
                pe.sem_inc(sem("group_mm"), 1)
                pe.wait_ge(sem("acc"), EACH["acc"] * l + 2 * g + 2)
            pe.wait_ge(sem("ada_row"), NX * (l + 2))
            for i in range(2 * (NG + 1)):
                g, tile = i // 2, i % 2
                ins = T.transpose(bank[5 + i // 4][:, (i % 4) * P:(i % 4 + 1) * P], sel[:, tile, g, :], ident)
                if i % 4 == 3 or i == 2 * NG + 1:
                    ins.then_inc(sem("selT_mm"), 1)
            pe.wait_ge(sem("selT"), EACH["selT"] * l + 3)
            for i in range(4):
                tile, hf = i // 2, i % 2
                for g in range(NG + 1):
                    ins = mm(bank[i][:], selT[:, g, tile * P:(tile + 1) * P], acc[:, g, hf * 512:hf * 512 + 512], g == 0, g == NG)
                ins.then_inc(sem("y_mm"), 1)

        pe.wait_ge(sem("consts"), 16)
        for n in range(NX):
            pe.wait_ge(sem("ada_sum"), n + 1)
            if n:
                pe.wait_ge(sem("ada_row"), n)
            mm(bank[7][0:1, 0:UC], C["ones"][:, 0:1], ada_acc[:, n % 2, 0:UC], True, True).then_inc(sem("ada_mm"), 1)
        for l in range(2):
            transpose_h(2 * l)
            qkv(l)
            (diff_attention, stick_attention)[l]()
            projection(l)
            transpose_h(2 * l + 1)
            router(l)
            experts(l)
        if TWO:
            pe_second(pe, mm)


NAMES = (
    "x", "c", "norm1_g", "norm2_g", "ada_w", "ada_b", "diff_w_in", "diff_w_out", "diff_lambda_q1", "diff_lambda_k1",
    "diff_lambda_q2", "diff_lambda_k2", "diff_subln_g", "sb_w_in", "sb_w_out", "router_group_w", "router_group_b",
    "router_expert_w", "router_expert_b", "expert_w_gate", "expert_w_up", "expert_w_down", "final_norm_g", "c_2", "ctx_2",
    "c_ctx_2", "w_mod_2", "b_mod_2", "norm_g_2", "w_in_2", "w_fmix_2", "g_ln_g_2", "g_ws_2", "g_bs_2", "q_a_g_2", "w_uq_2",
    "kv_a_g_2", "w_ukv_2", "q_norm_g_2", "k_norm_g_2", "w_out_2",
)


def kernel(**inputs):
    import concourse.bacc as bacc
    from concourse.bass_utils import run_bass_kernel_spmd

    nc = bacc.Bacc("TRN2", target_bir_lowering=False, num_devices=1)
    arrays = {n: np.ascontiguousarray(inputs[n]) for n in NAMES}
    arrays.update(constants())
    a = {n: nc.dram_tensor("in_" + n, v.shape, mybir.dt.from_np(v.dtype), kind="ExternalInput").ap() for n, v in arrays.items()}
    out = nc.dram_tensor("out_x", (1, S, D), F32, kind="ExternalOutput").ap()
    build(nc, a, out)
    r = run_bass_kernel_spmd(nc, [{"in_" + n: v for n, v in arrays.items()}], core_ids=[0])
    return r.results[0]["out_x"]
```

```python
from contextlib import ExitStack

import concourse.bass as bass
import numpy as np
from concourse import mybir

F32 = mybir.dt.float32
I32 = mybir.dt.int32
ALU = mybir.AluOpType
ACT = mybir.ActivationFunctionType
AX = mybir.AxisListType

P = 128
D = 1024
S = 256
TT = S // P
KT = D // P
HEADS_D = 8
HEADS_S = 16
HD = 64
NG, NE = 4, 8
NX = NG * NE
FH = 512
FK = FH // P
RING = 6
SLOT = KT * 512
UC = 6 * D // NX
NBIG = -1e30
A_HEADS, A_QK, A_NOPE, A_ROPE, A_V = 8, 96, 64, 32, 64
IN_W = 2208
WORK = 19200

EACH = dict(qkv_mm=12, qkv=12, proj_mm=4, oT=4, y_mm=4, hover_mm=1, hover=2, wsl_mm=1, wsl=1, cnt=1, gather_mm=NG + 1, hcur=2 * NG + 2,
            gu=NX, silu=NX, hid=NX, hid_tr=NX, hidT=NX, acc=2 * NG + 1, selT_mm=3, selT=3, sel=TT, logits=1, og=1,
            rank_mm=1, gdiff=1, ediff=1, r_exp=2)
EACH.update({n: 2 * A_HEADS * TT for n in ("a_s", "a_max", "a_exp", "a_tr", "a_pT", "a_pv", "a_o")})
EACH.update({n: 4 * TT for n in ("tok", "u_mm", "u_ss", "u_rms", "u_n", "u_tr", "uT")})
EACH.update(h2=2 * TT, h2T_mm=KT, h2T=KT, in_mm=10 * TT, proj=10 * TT, c_ss=1, c_rms=1, c_n=2 * TT, c_mm=1, cT=1,
            v_ss=1, v_rms=1, v_n=2 * TT, ws_mm=1, wsT=1, fa_mm=2, fa=2, ft_mm=2, ft=2, fm_mm=2, f_out=2, sg_mm=1, g_out=1,
            mixT_mm=8, mixT=8, out_mm=4 * TT, out_used=4 * TT - 1)

CONST_COLS = (("ident", P), ("suffix", P), ("minus", P), ("ones", P), ("before", P), ("iota", P), ("iota_over", P),
              ("dist0", P), ("dist1", S), ("strict", 3 * P), ("prio4", NG), ("prio8", NE))
CONST_W = sum(w for _, w in CONST_COLS)
CONST2_COLS = (("rope_cos", TT * A_ROPE), ("rope_sin", TT * A_ROPE), ("dft_cos", TT * S), ("dft_sin", TT * S),
               ("grp_cos", P), ("grp_sin", P))
CONST2_W = sum(w for _, w in CONST2_COLS)


def constants():
    i, j = np.arange(P)[:, None], np.arange(P)[None, :]
    k = np.arange(S)[None, :]

    def dist(q, k):
        return np.where(k // 64 <= q // 64, -np.abs(q - k), NBIG)

    strict = np.concatenate([j > i, np.ones((P, P)), j > i], 1)
    row = np.ones((P, 1))
    parts = dict(ident=i == j, suffix=-(i >= j).astype(float), minus=-np.ones((P, P)), ones=np.ones((P, P)), before=i < j,
                 iota=row * j, iota_over=row * (j + P), dist0=dist(i, j), dist1=dist(i + P, k), strict=strict,
                 prio4=row * (NG - np.arange(NG)), prio8=row * (NE - np.arange(NE)))
    first = np.concatenate([np.asarray(parts[n], np.float32) for n, _ in CONST_COLS], 1)
    pos = np.arange(S)
    half = A_ROPE // 2
    inv = (np.float32(10000.0) ** (-np.arange(0, half, 2, dtype=np.float32) / np.float32(half))).astype(np.float32)
    ar, ac = (pos // 64).astype(np.float32)[:, None] * inv, (pos % 64).astype(np.float32)[:, None] * inv
    ang = np.concatenate([ar, ar, ac, ac], 1)
    sign = np.repeat([-1.0, 1.0, -1.0, 1.0], A_ROPE // 4)
    tok = lambda a: np.asarray(a).reshape(TT, P, -1).transpose(1, 0, 2).reshape(P, -1)
    th = 2 * np.pi * ((pos[:, None] * pos[None, :]) % S) / S
    f = np.arange(HD)
    tf = 2 * np.pi * ((f[:, None] * f[None, :]) % HD) / HD
    scale = 1.0 / np.sqrt(S * HD)
    two = np.eye(2)
    second = np.concatenate([tok(np.cos(ang)), tok(np.sin(ang) * sign), tok(np.cos(th)), tok(np.sin(th)),
                             np.kron(two, np.cos(tf)) * scale, -np.kron(two, np.sin(tf)) * scale], 1)
    return {"consts": first.astype(np.float32), "consts2": second.astype(np.float32)}


class Chain:

    def __init__(self, eng, sem):
        self.eng, self.sem, self.n = eng, sem, 0

    def __call__(self, ins):
        self.n += 1
        ins.then_inc(self.sem, 1)
        self.eng.wait_ge(self.sem, self.n)


def build(nc, a, out):
    ctx = ExitStack()
    sb = lambda name, shape, dt=F32: ctx.enter_context(nc.sbuf_tensor(name, shape, dt))
    sems = {}

    def sem(name):
        if name not in sems:
            sems[name] = ctx.enter_context(nc.semaphore(name))
        return sems[name]

    with ctx:
        program(nc, a, out, sb, sem, ctx)


def program(nc, a, out, sb, sem, ctx):
    ring = sb("ring", [P, RING, SLOT])
    cst = sb("cst", [P, CONST_W])
    x = sb("x", [P, TT, D])
    rows = sb("rows", [P, 5, D])
    work = sb("work", [P, WORK])
    small = sb("small", [P, 512])
    cnt = sb("cnt", [1, 8], I32)
    psum = ctx.enter_context(nc.psum_tensor("psum", [P, 8, 512], F32))
    bank = [psum[:, i, :] for i in range(8)]
    mod = nc.dram_tensor("mod_scratch", (24, D), F32, kind="Internal").ap()
    modf = mod.rearrange("r (o n) -> o (r n)", o=1)

    C, at = {}, 0
    for name, w in CONST_COLS:
        C[name] = cst[:, at:at + w]
        at += w
    ident = C["ident"]
    hide = cst[:, 7 * P:10 * P]

    class Carver:

        def __init__(self, start=0):
            self.at = start

        def __call__(self, *shape):
            n = int(np.prod(shape))
            v = work[:, self.at:self.at + n]
            self.at += n
            assert self.at <= WORK, self.at
            names = "abcd"[:len(shape)]
            if len(shape) == 1:
                return v
            return v.rearrange(f"p ({' '.join(names)}) -> p {' '.join(names)}", **dict(zip(names[1:], shape[1:])))

    carve = Carver()
    ada_w = carve(2, KT * UC)
    ada_prod = carve(KT * UC)
    ada_acc = carve(2, 2 * UC)
    ada_row = carve(2, 2 * UC)
    ada_bias = carve(2, UC)
    base = carve.at
    AB = 4
    ada0 = ring[:, 4:6, :].rearrange("p r n -> p (r n)")[:, 0:AB * KT * UC].rearrange("p (b t n) -> p b t n", b=AB, t=KT)
    bias0 = work[0:1, base + 4 * D:base + 10 * D]
    cond = small[:, 0:24].rearrange("p (c t) -> p c t", c=3)
    ss = small[:, 24:26]
    rstd = small[:, 26:28]
    lam = small[:, 28:29]
    lvec = small[:, 32:36]

    carve = Carver(base)
    h = carve(TT, D)
    hT = carve(KT, S)
    qT = carve(KT, S)
    kT = carve(KT, S)
    v = carve(TT, D)
    att = carve.at
    oT = hT
    o = h
    sc_ = carve(2, 2, S)
    hf_ = hT.rearrange("p a b -> p (a b)")
    sc_ = [sc_[:, 0], sc_[:, 1], hf_[:, 0:2 * S].rearrange("p (m k) -> p m k", m=2)]
    aw = carve(2, S)
    awT = carve(2, 2, P)
    aw = [aw[:, 0], aw[:, 1], hf_[:, 2 * S:3 * S]]
    awT = [awT[:, 0], awT[:, 1], hf_[:, 3 * S:4 * S].rearrange("p (k q) -> p k q", k=2)]
    lqk = carve(4, HD)
    sub_g = carve(P)
    carve = Carver(att)
    sb_t = carve(2, 384)
    sb_e = sb_t
    sb_sp = carve(2, 384)
    sb_a = carve(2, 384)
    carve = Carver(base + TT * D)
    acc = carve(NG + 1, D)
    sel = carve(TT, NG + 1, P)
    selT_at = carve.at
    hcur = carve(KT, P)
    hover = carve(KT, P)
    selT = Carver(selT_at)(NG + 1, S)
    s_act = carve(FH)
    hid = carve(FH)
    hidT = carve(FK, P)
    wsl = carve(2 * NX)
    carve = Carver(base + TT * D + 2 * D)
    r_w = carve(KT, NG + NX)
    r_b = carve(NG + NX)
    rt = carve(640)

    class Cut:
        def __init__(self):
            self.at = 0

        def __call__(self, *shape):
            n = int(np.prod(shape))
            t = rt[:, self.at:self.at + n]
            self.at += n
            names = "abc"[:len(shape)]
            return t if len(shape) == 1 else t.rearrange(f"p ({' '.join(names)}) -> p {' '.join(names)}",
                                                         **dict(zip(names[1:], shape[1:])))

    cut = Cut()
    g4, g4b, g4c, og, eg = (cut(TT, NG) for _ in range(5))
    e32, e32b, w32 = (cut(TT, NX) for _ in range(3))
    e8, e8b, o1, o2, t8 = (cut(TT, NE) for _ in range(5))
    gm, pm, gs, m1, m2, ex, den, w1, w2, rk = (cut(TT) for _ in range(10))
    ogs = cut(NG)
    rkt = cut(TT, NG)

    loads = ["diff_w_in"] * 6 + ["diff_w_out"] * 2, ["sb_w_in"] * 6 + ["sb_w_out"] * 2
    L_BASE = [0, 8 + 3 * NX]
    M_BASE = [8, 16 + 3 * NX]

    def slot(n):
        return n % RING

    def loaded(eng, n, g=None):
        eng.wait_ge(sem(f"loaded{slot(n)}"), 16 * (n // RING + 1) if g is None else (n // RING + 1) * 16 + g * 64)

    def free(n):
        return sem(f"used{slot(n)}")

    def wslot(n, rows_, cols):
        return ring[:, slot(n), :].rearrange("p (t n) -> p t n", t=rows_)[:, :, 0:cols] if cols else None

    block = ctx.enter_context(nc.Block())

    ST = 2 * TT
    SECTIONS = {"f": (0, 512), "gv": (512, 512), "gq": (1024, 512), "kv": (1536, 160), "a": (1696, 512)}
    ORDER = (("gq", "kv", "gv", "f", "a"), ("kv", "gq", "gv", "f", "a"))
    tail = ring[:, 3:RING, :].rearrange("p r n -> p (r n)")
    t_at = [0]

    def cut2(*shape):
        n = int(np.prod(shape))
        t = tail[:, t_at[0]:t_at[0] + n]
        t_at[0] += n
        assert t_at[0] <= 3 * SLOT
        names = "abc"[:len(shape)]
        return t if len(shape) == 1 else t.rearrange(f"p ({' '.join(names)}) -> p {' '.join(names)}",
                                                     **dict(zip(names[1:], shape[1:])))

    y = cut2(TT, D)
    cst2 = cut2(CONST2_W)
    w_uq, w_ukv, w_fm, w_gs = cut2(2, 768), cut2(1024), cut2(2, 256), cut2(4, P)
    qa_g, kva_g, qn_g, kn_g, ln_g = cut2(256), cut2(P), cut2(A_QK), cut2(A_QK), cut2(HD)
    kT2 = cut2(A_HEADS, 2 * S)
    h2 = kT2.rearrange("p a b -> p (a b)").rearrange("p (t d) -> p t d", t=ST)
    carve = Carver(0)
    hT2 = carve(KT, 2 * S)
    proj = carve(ST, IN_W)
    qT2 = carve(A_HEADS, 2 * S)
    v2 = carve(ST, A_HEADS, A_V)
    rows_y = qT2.rearrange("p a b -> p (a b)")[:, 0:2 * D].rearrange("p (r d) -> p r d", r=2)
    mixT = hT2
    hflat = hT2.rearrange("p a b -> p (a b)")
    cqT = hflat[:, 0:1024].rearrange("p (c s) -> p c s", c=2)
    ckvT = hflat[:, 1024:1536]
    tok = [t_.rearrange("p (h e) -> p h e", h=A_HEADS) for t_ in (hflat[:, 1536:2304], hflat[:, 2304:3072], rows[:, 0, 0:768])]
    sqr = hflat[:, 3072:3840].rearrange("p (h e) -> p h e", h=A_HEADS)
    rot = hflat[:, 3840:4096].rearrange("p (h e) -> p h e", h=A_HEADS)
    pe_ = hflat[:, 0:1536].rearrange("p (b k) -> p b k", b=3)
    pT = hflat[:, 1536:3072].rearrange("p (b k q) -> p b k q", b=3, q=P)
    FT = rows[:, 1, 512:1024].rearrange("p (c s) -> p c s", c=2)
    wsT = rows[:, 1, 0:512].rearrange("p (h q) -> p h q", h=4)
    AT = rows[:, 2, :].rearrange("p (k c s) -> p k c s", k=2, c=2)
    C2, at = {}, 0
    for name, w in CONST2_COLS:
        C2[name] = cst2[:, at:at + w]
        at += w
    rope_c = C2["rope_cos"].rearrange("p (t e) -> p t e", t=TT)
    rope_s = C2["rope_sin"].rearrange("p (t e) -> p t e", t=TT)
    dft = [C2[n_].rearrange("p (t s) -> p t s", t=TT) for n_ in ("dft_cos", "dft_sin")]
    ss2, rs2 = small[:, 100:104], small[:, 104:108]
    ssc, rsc = small[:, 108:116], small[:, 116:124]
    ssh, rsh = ([small[:, at_ + 8 * k:at_ + 8 * k + 8] for k in range(2)] for at_ in (310, 326))
    bs = small[:, 140:144]
    bsr = small[0:4, 144:272]
    lm, lr = small[:, 272:288], small[:, 288:304]
    nm2, sm2, ri2 = small[:, 352:355], small[:, 356:360], small[:, 360:364]
    stream = lambda i: y[:, i, :] if i < TT else x[:, i - TT, :]

    def fills(l):
        return [(s_, i) for s_ in ORDER[l] for i in range(ST) if l == 0 or i >= TT or s_ == "kv"]

    def fills_through(l, s_):
        return max(n for n, f in enumerate(fills(l)) if f[0] == s_) + 1

    def out_fills(l):
        return [(hf, i) for hf in range(2) for i in range(0 if l == 0 else TT, ST)]

    def weights2():
        r = []
        for l in range(2):
            r += [(l, s_, "in_mm", EACH["in_mm"] * l + fills_through(l, s_)) for s_ in ORDER[l]]
            r += [(l, hf, "out_mm", EACH["out_mm"] * l + len(out_fills(l)) // 2 * (hf + 1)) for hf in range(2)]
        return r

    def units(l):
        return [(k, i) for i in range(ST) for k in range(2) if not (l and k and i < TT)]

    def attn(l):
        return [(s_, hd, qt) for s_ in range(l, 2) for hd in range(A_HEADS) for qt in range(TT)]

    def small_weights(eng, l, name):
        put = lambda dst, src, s_: eng.dma_start(dst, src).then_inc(sem(s_), 16)
        put(w_uq, a["w_uq_2"][l].rearrange("(c p) n -> p c n", p=P), name)
        put(w_ukv, a["w_ukv_2"][l], name)
        put(w_fm, a["w_fmix_2"][l].rearrange("(c p) n -> p c n", p=P), name)
        put(w_gs, a["g_ws_2"][l].rearrange("h p q -> p h q"), name)
        put(bsr, a["g_bs_2"][l], name)
        for t_, src in ((qa_g, "q_a_g_2"), (kva_g, "kv_a_g_2"), (qn_g, "q_norm_g_2"), (kn_g, "k_norm_g_2"),
                         (ln_g, "g_ln_g_2")):
            put(t_, a[src][l:l + 1, :].to_broadcast((P, a[src].shape[1])), name)

    def sp_second(sp):
        sp.wait_ge(sem("y_mm"), 8)
        sp.dma_start(y, a["ctx_2"][0].rearrange("(t p) d -> p t d", p=P)).then_inc(sem("y_in"), 16)
        for n, (l, what, _, _) in enumerate(weights2()):
            if n == 0:
                sp.wait_ge(sem("rows2_in"), 16 * 5)
            if n >= 3:
                _, _, s_, val = weights2()[n - 3]
                sp.wait_ge(sem(s_), val)
            if isinstance(what, str):
                c0, w = SECTIONS[what]
                src = a["w_in_2"][l][:, c0:c0 + w].rearrange("(p t) n -> p t n", t=KT)
            else:
                w = 512
                src = a["w_out_2"][l][:, what * 512:(what + 1) * 512].rearrange("(t p) n -> p t n", t=KT)
            sp.dma_start(ring[:, n % 3, 0:KT * w].rearrange("p (t n) -> p t n", t=KT), src).then_inc(sem(f"in2_{n % 3}"), 16)
            if n == 2:
                sp.dma_start(cst2, a["consts2"]).then_inc(sem("small_in"), 16)
                small_weights(sp, 0, "small_in")
        sp.wait_ge(sem("x_done"), 7)
        sp.dma_start(out[0].rearrange("(t p) d -> p t d", p=P), x[:]).then_inc(sem("out"), 16)
        sp.wait_ge(sem("out"), 16)

    def pool_second(pool):
        def get(dst, src, s_):
            pool.dma_start(dst, src).then_inc(sem(s_), 16)

        def row(k, l, r):
            n = 12 + k * 6 + l * 3 + r
            return mod[n:n + 1, :].to_broadcast((P, D))

        for l in range(2):
            if l:
                pool.wait_ge(sem("f_out"), 2)
                pool.wait_ge(sem("g_out"), 1)
                small_weights(pool, 1, "pool_weights")
            get(rows[:, 0, :], row(0, l, 1), "rows2_in")
            get(rows[:, 1, :], row(0, l, 0), "rows2_in")
            get(rows[:, 2, :], a["norm_g_2"][l:l + 1, :].to_broadcast((P, D)), "rows2_in")
            pool.wait_ge(*((sem("a_o"), 32) if l else (sem("y_mm"), 8)))
            get(rows_y[:, 0, :], row(1, l, 1), "rows2_in")
            get(rows_y[:, 1, :], row(1, l, 0), "rows2_in")
            pool.wait_ge(sem("x_done"), 5 + l)
            get(rows[:, 3, :], row(0, l, 2), "gates2_in")
            get(rows[:, 4, :], row(1, l, 2), "gates2_in")

    def stream_rms(act, link, s_, l):
        if s_ == 0 and l == 0:
            act.wait_ge(sem("y_in"), 16)
        else:
            act.wait_ge(sem("x_done"), 5 + l)
        for i in range(TT * s_, TT * s_ + TT):
            link(nc.scalar.activation(h2[:, i, :], stream(i), ACT.Square, accum_out=ss2[:, i:i + 1]))
        part = slice(TT * s_, TT * s_ + TT)
        nc.scalar.activation(rs2[:, part], ss2[:, part], ACT.Sqrt, scale=1.0 / D, bias=small[:, 40:41]).then_inc(sem("rms"), 1)

    def stream_norm(dve, link, s_, l):
        V = nc.vector
        if s_ == 0:
            dve.wait_ge(sem("rows2_in"), 16 * 5 * (l + 1))
            link(V.scalar_tensor_tensor(rows_y[:, 0, :], rows_y[:, 0, :], 1.0, rows[:, 2, :], ALU.add, ALU.mult))
            link(V.scalar_tensor_tensor(rows[:, 0, :], rows[:, 0, :], 1.0, rows[:, 2, :], ALU.add, ALU.mult))
        dve.wait_ge(sem("rms"), 8 + s_ if l else 5 + 2 * s_)
        part = slice(TT * s_, TT * s_ + TT)
        link(V.reciprocal(rs2[:, part], rs2[:, part]))
        gain, shift = (rows[:, 0, :], rows[:, 1, :]) if s_ else (rows_y[:, 0, :], rows_y[:, 1, :])
        for i in range(TT * s_, TT * s_ + TT):
            link(V.scalar_tensor_tensor(h2[:, i, :], stream(i), rs2[:, i:i + 1], gain, ALU.mult, ALU.mult))
            V.tensor_tensor(h2[:, i, :], h2[:, i, :], shift, ALU.add).then_inc(sem("h2"), 1)

    def act_second(act, link, copy):
        def sqrt(dst, src, n, done):
            nc.scalar.activation(dst, src, ACT.Sqrt, scale=1.0 / n, bias=small[:, 40:41]).then_inc(sem(done), 1)

        for l in range(2):
            if l:
                stream_rms(act, link, 0, 1)
            for k in range(2):
                if k == 0 and l:
                    stream_rms(act, link, 1, l)
                if k and l == 0:
                    stream_rms(act, link, 1, l)
                for t in range(0, KT, 2):
                    act.wait_ge(sem("h2T_mm"), EACH["h2T_mm"] * l + k * KT // 2 + t // 2 + 1)
                    copy(hT2[:, t:t + 2, k * S:(k + 1) * S], bank[4 + t // 2].rearrange("p (t n) -> p t n", t=2)).then_inc(
                        sem("h2T"), 1)
            for n, (s_, i) in enumerate(fills(l)):
                act.wait_ge(sem("in_mm"), EACH["in_mm"] * l + n + 1)
                c0, w = SECTIONS[s_]
                src = bank[n % 4]
                half = w // 2
                if s_ == "a":
                    ins = nc.scalar.activation(proj[:, i, c0:c0 + w], src, ACT.Silu)
                elif s_ in ("f", "gq"):
                    lo = s_ == "gq"
                    link(nc.scalar.activation(proj[:, i, c0:c0 + half], src[:, 0:half], ACT.Silu if lo else ACT.Copy))
                    ins = nc.scalar.activation(proj[:, i, c0 + half:c0 + w], src[:, half:w], ACT.Copy if lo else ACT.Silu)
                else:
                    ins = copy(proj[:, i, c0:c0 + w], src[:, 0:w])
                ins.then_inc(sem("proj"), 1)
                if n + 1 == fills_through(l, "f"):
                    act.wait_ge(sem("c_ss"), EACH["c_ss"] * l + 1)
                    link(nc.scalar.activation(rsc[:, 0:4], ssc[:, 0:4], ACT.Sqrt, scale=1.0 / 256, bias=small[:, 40:41]))
                    sqrt(rsc[:, 4:8], ssc[:, 4:8], P, "c_rms")
                    act.wait_ge(sem("v_ss"), EACH["v_ss"] * l + 1)
                    sqrt(lr, lr, HD, "v_rms")
            act.wait_ge(sem("c_mm"), EACH["c_mm"] * l + 1)
            for c in range(2):
                link(copy(cqT[:, c, :], bank[c]))
            copy(ckvT, bank[2]).then_inc(sem("cT"), 1)
            act.wait_ge(sem("ws_mm"), EACH["ws_mm"] * l + 1)
            link(copy(wsT.rearrange("p h q -> p (h q)"), bank[6]))
            copy(bs, bank[7][:, 0:4]).then_inc(sem("wsT"), 1)
            U = units(l)

            def take_fourier(step):
                o = step // 3
                if step % 3 == 0:
                    act.wait_ge(sem("fa_mm"), EACH["fa_mm"] * l + o + 1)
                    link(copy(AT[:, 0], bank[6].rearrange("p (c s) -> p c s", c=2)))
                    copy(AT[:, 1], bank[7].rearrange("p (c s) -> p c s", c=2)).then_inc(sem("fa"), 1)
                elif step % 3 == 1:
                    act.wait_ge(sem("ft_mm"), EACH["ft_mm"] * l + o + 1)
                    copy(FT, bank[6].rearrange("p (c s) -> p c s", c=2)).then_inc(sem("ft"), 1)

            def take_unit(n):
                k, i = U[n]
                b = 2 * (n % 2)
                t_ = tok[n % 3]
                act.wait_ge(sem("u_mm"), EACH["u_mm"] * l + n + 1)
                if k:
                    ins = copy(t_.rearrange("p (b h) e -> p b (h e)", b=2), psum[:, b:b + 2, 0:384])
                else:
                    kv = psum[:, b:b + 2, :].rearrange("p b (h e) -> p (b h) e", h=4)
                    link(copy(t_[:, :, 0:A_NOPE], kv[:, :, 0:A_NOPE]))
                    link(copy(v2[:, i], kv[:, :, A_NOPE:]))
                    ins = copy(t_[:, :, A_NOPE:], proj[:, i, 1664:1696].unsqueeze(1).to_broadcast((P, A_HEADS, A_ROPE)))
                ins.then_inc(sem("tok"), 1)

            def unit_rms(n):
                act.wait_ge(sem("u_ss"), EACH["u_ss"] * l + n + 1)
                sqrt(rsh[n % 2], ssh[n % 2], A_QK, "u_rms")

            take_unit(0)
            take_unit(1)
            unit_rms(0)
            for n, (k, i) in enumerate(U):
                if n + 2 < len(U):
                    take_unit(n + 2)
                if n + 1 < len(U):
                    unit_rms(n + 1)
                if 0 < n <= 3 * (2 - l):
                    take_fourier(n - 1)
                act.wait_ge(sem("u_tr"), EACH["u_tr"] * l + n + 1)
                copy((kT2, qT2)[k][0:A_QK, :, i * P:(i + 1) * P],
                     psum[0:A_QK, 4:6, :].rearrange("p b (h s) -> p (b h) s", h=4)).then_inc(sem("uT"), 1)
            A = attn(l)
            for k in range(len(A) + 2):
                if k < len(A):
                    nk = (2 + 2 * A[k][0]) * P
                    act.wait_ge(sem("a_max"), EACH["a_max"] * l + k + 1)
                    if k >= 4:
                        act.wait_ge(sem("a_o"), EACH["a_o"] * l + k - 3)
                    nc.scalar.activation(pe_[:, k % 3, 0:nk], bank[k % 3][:, 0:nk], ACT.Exp, bias=nm2[:, k % 3:k % 3 + 1],
                                         accum_out=sm2[:, k % 4:k % 4 + 1]).then_inc(sem("a_exp"), 1)
                if k >= 2:
                    u = k - 2
                    n = 2 + 2 * A[u][0]
                    act.wait_ge(sem("a_tr"), EACH["a_tr"] * l + u + 1)
                    copy(pT[:, u % 3, 0:n, :], bank[3 + u % 2][:, 0:n * P].rearrange("p (k q) -> p k q", k=n)).then_inc(
                        sem("a_pT"), 1)
            for c in range(8):
                act.wait_ge(sem("mixT_mm"), EACH["mixT_mm"] * l + c + 1)
                lo = 0 if l == 0 else S
                copy(mixT[:, c, lo:2 * S], bank[c][:, lo:2 * S]).then_inc(sem("mixT"), 1)

    def dve_second(dve, link):
        V = nc.vector
        for l in range(2):
            if l:
                stream_norm(dve, link, 0, 1)
            stream_norm(dve, link, 1, l)
            dve.wait_ge(sem("h2"), EACH["h2"] * l + ST)
            dve.wait_ge(sem("proj"), EACH["proj"] * l + max(fills_through(l, "gq"), fills_through(l, "kv")))
            q0 = 0 if l == 0 else TT
            nq = ST - q0
            cq, ckv = proj[:, q0:, 1280:1536], proj[:, :, 1536:1664]
            sq = qT2.rearrange("p a b -> p (a b)")
            sq_q = sq[:, 0:nq * 256].rearrange("p (t n) -> p t n", t=nq)
            sq_k = sq[:, 1024:1536].rearrange("p (t n) -> p t n", t=ST)
            if l:
                link(V.memset(ssc[:, 0:TT], 0.0))
            link(V.tensor_tensor(sq_q, cq, cq, ALU.mult))
            link(V.tensor_reduce(ssc[:, q0:ST], sq_q, AX.X, ALU.add))
            link(V.tensor_tensor(sq_k, ckv, ckv, ALU.mult))
            V.tensor_reduce(ssc[:, 4:8], sq_k, AX.X, ALU.add).then_inc(sem("c_ss"), 1)
            dve.wait_ge(sem("proj"), EACH["proj"] * l + fills_through(l, "gv"))
            gv = [proj[:, i, 768:1024].rearrange("p (h e) -> p h e", h=4) for i in range(q0, ST)]
            sq_v = [sq[:, 2048 + 256 * i:2304 + 256 * i].rearrange("p (h e) -> p h e", h=4) for i in range(nq)]
            if l:
                link(V.memset(lr, 1.0))
            for i, g_ in enumerate(gv):
                m_, r_ = lm[:, 4 * i:4 * i + 4], lr[:, 4 * i:4 * i + 4]
                link(V.tensor_reduce(m_, g_, AX.X, ALU.add))
                link(V.tensor_scalar(m_, m_, 1.0 / HD, None, ALU.mult))
                link(V.tensor_tensor(g_, g_, m_.unsqueeze(2).to_broadcast((P, 4, HD)), ALU.subtract))
                link(V.tensor_tensor(sq_v[i], g_, g_, ALU.mult))
                ins = V.tensor_reduce(r_, sq_v[i], AX.X, ALU.add)
                if i < nq - 1:
                    link(ins)
            ins.then_inc(sem("v_ss"), 1)
            dve.wait_ge(*((sem("pool_weights"), 128 + 160) if l else (sem("small_in"), 176)))
            dve.wait_ge(sem("c_rms"), EACH["c_rms"] * l + 1)
            link(V.reciprocal(rsc, rsc))
            for i in range(ST):
                if i >= q0:
                    link(V.scalar_tensor_tensor(proj[:, i, 1280:1536], proj[:, i, 1280:1536], rsc[:, i:i + 1], qa_g, ALU.mult, ALU.mult))
                V.scalar_tensor_tensor(proj[:, i, 1536:1664], proj[:, i, 1536:1664], rsc[:, 4 + i:5 + i], kva_g,
                                       ALU.mult, ALU.mult).then_inc(sem("c_n"), 1)
            dve.wait_ge(sem("v_rms"), EACH["v_rms"] * l + 1)
            link(V.reciprocal(lr, lr))
            for i, g_ in enumerate(gv):
                link(V.tensor_tensor(g_, g_, lr[:, 4 * i:4 * i + 4].unsqueeze(2).to_broadcast((P, 4, HD)), ALU.mult))
                V.tensor_tensor(g_, g_, ln_g.unsqueeze(1).to_broadcast((P, 4, HD)), ALU.mult).then_inc(sem("v_n"), 1)
            link(V.tensor_scalar(qn_g, qn_g, A_QK ** -0.5, None, ALU.mult))
            U = units(l)

            def fourier_gate(o):
                dve.wait_ge(sem("fm_mm"), EACH["fm_mm"] * l + o + 1)
                s_ = l + o
                V.tensor_tensor(proj[:, 2 * s_:2 * s_ + 2, 0:256], bank[7].rearrange("p (t n) -> p t n", t=2),
                                proj[:, 2 * s_:2 * s_ + 2, 256:512], ALU.mult).then_inc(sem("f_out"), 1)

            def unit_squares(n):
                dve.wait_ge(sem("tok"), EACH["tok"] * l + n + 1)
                link(V.tensor_tensor(sqr, tok[n % 3], tok[n % 3], ALU.mult))
                V.tensor_reduce(ssh[n % 2], sqr, AX.X, ALU.add).then_inc(sem("u_ss"), 1)
                dve.wait_ge(sem("u_ss"), EACH["u_ss"] * l + n + 1)

            def unit_norm(n):
                k, i = U[n]
                t_ = tok[n % 3]
                dve.wait_ge(sem("u_rms"), EACH["u_rms"] * l + n + 1)
                link(V.reciprocal(rsh[n % 2], rsh[n % 2]))
                link(V.tensor_tensor(t_, t_, rsh[n % 2].unsqueeze(2).to_broadcast((P, A_HEADS, A_QK)), ALU.mult))
                ins = V.tensor_tensor(t_, t_, (kn_g, qn_g)[k].unsqueeze(1).to_broadcast((P, A_HEADS, A_QK)), ALU.mult)
                if i >= TT:
                    link(ins)
                    r_ = t_[:, :, A_NOPE:]
                    r4 = r_.rearrange("p h (a b c) -> p h a b c", a=2, b=2)
                    o4_ = rot.rearrange("p h (a b c) -> p h a b c", a=2, b=2)
                    s4 = rope_s[:, i - TT, :].rearrange("p (a b c) -> p a b c", a=2, b=2)
                    for b in range(2):
                        ins = V.tensor_tensor(o4_[:, :, :, b, :], r4[:, :, :, 1 - b, :],
                                              s4[:, :, b, :].unsqueeze(1).to_broadcast((P, A_HEADS, 2, 8)), ALU.mult)
                        if b:
                            link(ins)
                    link(V.tensor_tensor(r_, r_, rope_c[:, i - TT, :].unsqueeze(1).to_broadcast((P, A_HEADS, A_ROPE)), ALU.mult))
                    ins = V.tensor_tensor(r_, r_, rot, ALU.add)
                ins.then_inc(sem("u_n"), 1)
                dve.wait_ge(sem("u_n"), EACH["u_n"] * l + n + 1)

            unit_squares(0)
            unit_squares(1)
            unit_norm(0)
            for n in range(2, len(U) + 1):
                if n < len(U):
                    unit_squares(n)
                unit_norm(n - 1)
                if n == 4:
                    fourier_gate(0)
            if l == 0:
                fourier_gate(1)
            dve.wait_ge(sem("sg_mm"), EACH["sg_mm"] * l + 1)
            for hd in range(4):
                u_ = proj[:, q0:, 512 + hd * HD:512 + (hd + 1) * HD]
                src = bank[6 + hd // 2][:, (hd % 2) * 256:(hd % 2) * 256 + nq * HD].rearrange("p (t e) -> p t e", t=nq)
                link(V.scalar_tensor_tensor(u_, src, bs[:, hd:hd + 1], u_, ALU.add, ALU.mult))
            V.tensor_tensor(proj[:, q0:, 512:768], proj[:, q0:, 512:768], proj[:, q0:, 1024:1280], ALU.mult).then_inc(
                sem("g_out"), 1)
            A = attn(l)
            for k in range(len(A) + 3):
                if k < len(A):
                    nk = (2 + 2 * A[k][0]) * P
                    dve.wait_ge(sem("a_s"), EACH["a_s"] * l + k + 1)
                    if k >= 3:
                        dve.wait_ge(sem("a_exp"), EACH["a_exp"] * l + k - 2)
                    V.tensor_reduce(nm2[:, k % 3:k % 3 + 1], bank[k % 3][:, 0:nk], AX.X, ALU.max, negate=True).then_inc(
                        sem("a_max"), 1)
                if k >= 3:
                    u = k - 3
                    s_, hd, qt = A[u]
                    dve.wait_ge(sem("a_pv"), EACH["a_pv"] * l + u + 1)
                    link(V.reciprocal(ri2[:, u % 4:u % 4 + 1], sm2[:, u % 4:u % 4 + 1]))
                    g_ = proj[:, 2 * s_ + qt, 1696 + hd * A_V:1696 + (hd + 1) * A_V]
                    V.scalar_tensor_tensor(g_, bank[5 + u % 2][:, 0:A_V], ri2[:, u % 4:u % 4 + 1], g_, ALU.mult, ALU.mult).then_inc(
                        sem("a_o"), 1)
                    dve.wait_ge(sem("a_o"), EACH["a_o"] * l + u + 1)
            tmp = qT2.rearrange("p a b -> p (a b)")[:, 2 * D:]
            F = out_fills(l)
            dve.wait_ge(sem("gates2_in"), 32 * (l + 1))
            for n, (hf, i) in enumerate(F):
                dve.wait_ge(sem("out_mm"), EACH["out_mm"] * l + n + 1)
                gate = rows[:, 4 if i < TT else 3, hf * 512:(hf + 1) * 512]
                dst = stream(i)[:, hf * 512:(hf + 1) * 512]
                if n >= 4:
                    dve.wait_ge(sem("out_used"), EACH["out_used"] * l + n - 3)
                link(V.tensor_tensor(tmp[:, n % 4 * 512:n % 4 * 512 + 512], bank[n % 4], gate, ALU.mult))
                ins = V.tensor_tensor(dst, dst, tmp[:, n % 4 * 512:n % 4 * 512 + 512], ALU.add)
                if n < len(F) - 1:
                    ins.then_inc(sem("out_used"), 1)
            ins.then_inc(sem("x_done"), 1)
            dve.wait_ge(sem("x_done"), 6 + l)

    def pe_second(pe, mm):
        T = nc.tensor
        for l in range(2):
            q0 = 0 if l == 0 else TT
            nq = ST - q0
            def turn_stream(k):
                for t in range(KT):
                    for i in range(TT):
                        ins = T.transpose(bank[4 + t // 2][:, (t % 2 * TT + i) * P:(t % 2 * TT + i + 1) * P],
                                          h2[:, TT * k + i, t:D:KT], ident)
                    if t % 2:
                        ins.then_inc(sem("h2T_mm"), 1)

            pe.wait_ge(sem("x_done"), 4 + 2 * l)
            pe.wait_ge(sem("h2"), EACH["h2"] * l + TT)
            turn_stream(0)
            W = weights2()
            pe.wait_ge(sem("h2T"), EACH["h2T"] * l + KT // 2)
            for n, (s_, i) in enumerate(fills(l)):
                if n == TT:
                    pe.wait_ge(sem("h2"), EACH["h2"] * l + ST)
                    turn_stream(1)
                    pe.wait_ge(sem("h2T"), EACH["h2T"] * l + KT)
                r = next(j for j, w in enumerate(W) if w[:2] == (l, s_))
                pe.wait_ge(sem(f"in2_{r % 3}"), 16 * (r // 3 + 1))
                if n >= 4:
                    pe.wait_ge(sem("proj"), EACH["proj"] * l + n - 3)
                w = SECTIONS[s_][1]
                wt = ring[:, r % 3, 0:KT * w].rearrange("p (t n) -> p t n", t=KT)
                for t in range(KT):
                    ins = mm(bank[n % 4][:, 0:w], hT2[:, t, i * P:(i + 1) * P], wt[:, t, :], t == 0, t == KT - 1)
                ins.then_inc(sem("in_mm"), 1)
            pe.wait_ge(*((sem("pool_weights"), 128 + 160) if l else (sem("small_in"), 176)))
            for hd in range(4):
                T.transpose(bank[6][:, hd * P:(hd + 1) * P], w_gs[:, hd, :], ident)
            T.transpose(bank[7][:, 0:4], bsr, ident[0:4, 0:4]).then_inc(sem("ws_mm"), 1)
            pe.wait_ge(sem("proj"), EACH["proj"] * l + len(fills(l)))
            pe.wait_ge(sem("c_n"), EACH["c_n"] * l + ST)
            for i in range(ST):
                if i >= q0:
                    for c in range(2):
                        T.transpose(bank[c][:, i * P:(i + 1) * P], proj[:, i, 1280 + c * P:1408 + c * P], ident)
                ins = T.transpose(bank[2][:, i * P:(i + 1) * P], proj[:, i, 1536:1664], ident)
            ins.then_inc(sem("c_mm"), 1)
            pe.wait_ge(sem("cT"), EACH["cT"] * l + 1)
            U = units(l)

            def unit(n):
                k, i = U[n]
                b = 2 * (n % 2)
                if n >= 2:
                    pe.wait_ge(sem("tok"), EACH["tok"] * l + n - 1)
                for j in range(2):
                    if k:
                        for c in range(2):
                            ins = mm(bank[b + j][:, 0:384], cqT[:, c, i * P:(i + 1) * P], w_uq[:, c, j * 384:(j + 1) * 384], c == 0, c == 1)
                    else:
                        ins = mm(bank[b + j], ckvT[:, i * P:(i + 1) * P], w_ukv[:, j * 512:(j + 1) * 512], True, True)
                ins.then_inc(sem("u_mm"), 1)

            def fourier(step):
                o = step // 3
                s_ = l + o
                if step % 3 == 0:
                    if o:
                        pe.wait_ge(sem("f_out"), EACH["f_out"] * l + o)
                    else:
                        pe.wait_ge(sem("wsT"), EACH["wsT"] * l + 1)
                    for k in range(2):
                        for c in range(2):
                            for t in range(TT):
                                ins = mm(bank[6 + k][:, c * S:(c + 1) * S], proj[:, 2 * s_ + t, c * P:(c + 1) * P], dft[k][:, t, :],
                                         t == 0, t == 1)
                    ins.then_inc(sem("fa_mm"), 1)
                elif step % 3 == 1:
                    pe.wait_ge(sem("fa"), EACH["fa"] * l + o + 1)
                    for c in range(2):
                        for k, g_ in enumerate(("grp_cos", "grp_sin")):
                            ins = mm(bank[6][:, c * S:(c + 1) * S], C2[g_], AT[:, k, c, :], k == 0, k == 1)
                    ins.then_inc(sem("ft_mm"), 1)
                else:
                    pe.wait_ge(sem("ft"), EACH["ft"] * l + o + 1)
                    for t in range(TT):
                        for c in range(2):
                            ins = mm(bank[7][:, t * 256:(t + 1) * 256], FT[:, c, t * P:(t + 1) * P], w_fm[:, c, :], c == 0, c == 1)
                    ins.then_inc(sem("fm_mm"), 1)

            unit(0)
            unit(1)
            for n in range(len(U)):
                if n + 2 < len(U):
                    unit(n + 2)
                if 0 < n <= 3 * (2 - l):
                    fourier(n - 1)
                pe.wait_ge(sem("u_n"), EACH["u_n"] * l + n + 1)
                if n:
                    pe.wait_ge(sem("uT"), EACH["uT"] * l + n)
                for hd in range(A_HEADS):
                    ins = T.transpose(bank[4 + hd // 4][0:A_QK, (hd % 4) * P:(hd % 4 + 1) * P], tok[n % 3][:, hd, :], ident)
                ins.then_inc(sem("u_tr"), 1)
            pe.wait_ge(sem("v_n"), EACH["v_n"] * l + nq)
            pe.wait_ge(sem("f_out"), EACH["f_out"] * l + 2 - l)
            for hd in range(4):
                ins = mm(bank[6 + hd // 2][:, (hd % 2) * 256:(hd % 2) * 256 + nq * HD], wsT[:, hd, :],
                         proj[:, q0:, 768 + hd * HD:768 + (hd + 1) * HD], True, True)
            ins.then_inc(sem("sg_mm"), 1)
            pe.wait_ge(sem("uT"), EACH["uT"] * l + len(U))
            pe.wait_ge(sem("fa"), EACH["fa"] * l + 2 - l)
            A = attn(l)
            for k in range(len(A) + 3):
                if k < len(A):
                    s_, hd, qt = A[k]
                    nk = (2 + 2 * s_) * P
                    if k >= 3:
                        pe.wait_ge(sem("a_exp"), EACH["a_exp"] * l + k - 2)
                    q_ = (2 * s_ + qt) * P
                    mm(bank[k % 3][:, 0:nk], qT2[0:A_QK, hd, q_:q_ + P], kT2[0:A_QK, hd, 0:nk], True, True).then_inc(sem("a_s"), 1)
                if 2 <= k < len(A) + 2:
                    u = k - 2
                    pe.wait_ge(sem("a_exp"), EACH["a_exp"] * l + u + 1)
                    if u >= 2:
                        pe.wait_ge(sem("a_pT"), EACH["a_pT"] * l + u - 1)
                    for j in range(2 + 2 * A[u][0]):
                        ins = T.transpose(bank[3 + u % 2][:, j * P:(j + 1) * P], pe_[:, u % 3, j * P:(j + 1) * P], ident)
                    ins.then_inc(sem("a_tr"), 1)
                if k >= 3:
                    u = k - 3
                    s_, hd, qt = A[u]
                    pe.wait_ge(sem("a_pT"), EACH["a_pT"] * l + u + 1)
                    if u >= 2:
                        pe.wait_ge(sem("a_o"), EACH["a_o"] * l + u - 1)
                    n = 2 + 2 * s_
                    for j in range(n):
                        ins = mm(bank[5 + u % 2][:, 0:A_V], pT[:, u % 3, j, :], v2[:, j, hd, :], j == 0, j == n - 1)
                    ins.then_inc(sem("a_pv"), 1)
            pe.wait_ge(sem("a_o"), EACH["a_o"] * l + len(A))
            pe.wait_ge(sem("g_out"), EACH["g_out"] * l + 1)
            pe.wait_ge(sem("f_out"), EACH["f_out"] * l + 2 - l)
            cols = [0, P, 512, 640, 1696, 1824, 1952, 2080]
            for c, col in enumerate(cols):
                for i in range(q0, ST):
                    ins = T.transpose(bank[c][:, i * P:(i + 1) * P], proj[:, i, col:col + P], ident)
                ins.then_inc(sem("mixT_mm"), 1)
            pe.wait_ge(sem("mixT"), EACH["mixT"] * l + 8)
            for n, (hf, i) in enumerate(out_fills(l)):
                r = next(j for j, w in enumerate(W) if w[0] == l and w[1] == hf and not isinstance(w[1], str))
                pe.wait_ge(sem(f"in2_{r % 3}"), 16 * (r // 3 + 1))
                if n >= 4:
                    pe.wait_ge(sem("out_used"), EACH["out_used"] * l + n - 3)
                wt = ring[:, r % 3, :].rearrange("p (t n) -> p t n", t=KT)
                for t in range(KT):
                    ins = mm(bank[n % 4], mixT[:, t, i * P:(i + 1) * P], wt[:, t, :], t == 0, t == KT - 1)
                ins.then_inc(sem("out_mm"), 1)

    @block.sync
    def _(sp):
        def room(n, g=None):
            if g is None:
                if n >= RING:
                    sp.wait_ge(free(n), n // RING)
            else:
                sp.wait_ge(free(n), n // RING + 4 * g)

        def ada_unit(l, u, g, w_ap, b_ap):
            sp.wait_ge(sem("ada_row"), NX * (l + 1) + g * NE + u - 1)
            sp.dma_start(ada_w[:, u % 2, :].rearrange("p (t n) -> p t n", t=KT), w_ap).then_inc(sem(f"ada_in{u % 2}"), 16)
            sp.dma_start(ada_bias[0:1, u % 2, :], b_ap).then_inc(sem(f"ada_in{u % 2}"), 16)

        ada = a["ada_w"]

        def ada_src(l, u, g):
            w = ada[l].rearrange("(p t) (g n) -> p t g n", t=KT, g=NG)
            b = a["ada_b"][l:l + 1, :].rearrange("a (g n) -> a g n", g=NG)
            c = u * UC
            if isinstance(g, int):
                return w[:, :, g, c:c + UC], b[:, g, c:c + UC]
            return (w[:, :, bass.ds(g, 1), c:c + UC].rearrange("p t g n -> p t (g n)"),
                    b[:, bass.ds(g, 1), c:c + UC].rearrange("a g n -> a (g n)"))

        def ada2_src(u, g):
            l, c = u // 4, (u % 4) * UC
            w = a["w_mod_2"][l].rearrange("(p t) (g n) -> p t g n", t=KT, g=NG)
            b = a["b_mod_2"][l:l + 1, :].rearrange("a (g n) -> a g n", g=NG)
            return (w[:, :, bass.ds(g, 1), c:c + UC].rearrange("p t g n -> p t (g n)"),
                    b[:, bass.ds(g, 1), c:c + UC].rearrange("a g n -> a (g n)"))

        def weight(l, n):
            room(L_BASE[l] + n)
            W = a[loads[l][n]][0]
            if n < 6:
                src = W[:, n * 512:(n + 1) * 512].rearrange("(p t) n -> p t n", t=KT)
            else:
                src = W[:, (n - 6) * 512:(n - 5) * 512].rearrange("(t p) n -> p t n", t=KT)
            sp.dma_start(wslot(L_BASE[l] + n, KT, 512), src).then_inc(sem(f"loaded{slot(L_BASE[l] + n)}"), 16)

        sp.dma_start(cst[:], a["consts"]).then_inc(sem("consts"), 16)
        for k, name in enumerate(("c", "c_2", "c_ctx_2")):
            src = a[name] if len(a[name].shape) == 2 else a[name].rearrange("(a n) -> a n", a=1)
            sp.dma_start(cond[:, k, :], src.rearrange("a (p t) -> p (a t)", p=P)).then_inc(sem("cond_in"), 16)
        sp.dma_start(x[:], a["x"][0].rearrange("(t p) d -> p t d", p=P)).then_inc(sem("x_in"), 16)
        sp.dma_start(bias0, a["ada_b"][0:1, :]).then_inc(sem("cond_in"), 16)
        for n in range(NX):
            if n >= AB:
                sp.wait_ge(sem("ada_mm"), n - AB + 1)
            sp.dma_start(ada0[:, n % AB], ada_src(0, n % NE, n // NE)[0]).then_inc(sem(f"start_in{n % AB}"), 16)
            if n >= NX - 4:
                weight(0, n - NX + 4)
        sp.wait_ge(sem("ada_mm"), NX)
        for l in range(2):
            for n in range(0 if l else 4, 8):
                weight(l, n)
            with sp.Fori(0, NG) as g:
                for e in range(NE):
                    ada_unit(l, e, g, *(ada_src(1, e, g) if l == 0 else ada2_src(e, g)))
                    for j, name in enumerate(("expert_w_gate", "expert_w_up", "expert_w_down")):
                        n = M_BASE[l] + 3 * e + j
                        room(n, g)
                        W = a[name][l].rearrange("(g e) k n -> g e k n", g=NG)[bass.ds(g, 1), e]
                        sp.dma_start(ring[:, slot(n), :], W.rearrange("g (p t) n -> p (g t n)", p=P)).then_inc(
                            sem(f"loaded{slot(n)}"), 16)
        sp_second(sp)

    @block.gpsimd
    def _(pool):
        def row_load(i, src):
            pool.dma_start(rows[:, i, :], src).then_inc(sem("rows_in"), 16)

        def store_unit(u, g, n, off, conds):
            pool.wait_ge(sem("ada_row"), n)
            for k in range(conds):
                dst = off(k)
                pool.dma_start(dst, ada_row[0:1, u % 2, k * UC:(k + 1) * UC]).then_inc(sem(f"ada_out{u % 2}"), 16)

        def first_dst(l, u, g):
            v_ = modf[:, l * 6 * D:(l + 1) * 6 * D].rearrange("o (g n) -> o g n", g=NG)
            if isinstance(g, int):
                return lambda k: v_[:, g, u * UC:(u + 1) * UC]
            return lambda k: v_[:, bass.ds(g, 1), u * UC:(u + 1) * UC].rearrange("o g n -> o (g n)")

        def second_dst(u, g):
            def off(k):
                lo = 12 * D + (k * 2 + u // 4) * 3 * D
                v_ = modf[:, lo:lo + 3 * D].rearrange("o (g n) -> o g n", g=NG)
                return v_[:, bass.ds(g, 1), (u % 4) * UC:(u % 4 + 1) * UC].rearrange("o g n -> o (g n)")
            return off

        def stage_rows(n):
            l, half = n // 2, n % 2
            for par in range(2):
                if n or par == 0:
                    pool.wait_ge(sem(f"ada_out{par}"), 16 * (1 + 16 * l))
            if n:
                pool.wait_ge(sem("h_done"), n)
            if n >= 2:
                pool.wait_ge(sem("x_done"), n - 1)
            r = 6 * l + 3 * half
            row_load(0, mod[r + 1:r + 2, :].to_broadcast((P, D)))
            row_load(1, mod[r:r + 1, :].to_broadcast((P, D)))
            row_load(2 if half == 0 else 4, mod[r + 2:r + 3, :].to_broadcast((P, D)))
            row_load(3, a["norm2_g" if half else "norm1_g"][l:l + 1, :].to_broadcast((P, D)))

        for half in range(2):
            pool.wait_ge(sem("ada_row"), NX // 2 * (half + 1))
            w = 3 * D
            pool.dma_start(modf[:, half * w:(half + 1) * w], bias0[:, half * w:(half + 1) * w]).then_inc(sem(f"ada_out{half}"), 16)
            if half == 0:
                stage_rows(0)
        for k, name in enumerate(("diff_lambda_q1", "diff_lambda_k1", "diff_lambda_q2", "diff_lambda_k2")):
            pool.dma_start(lqk[:, k, :], a[name][0:1, :].to_broadcast((P, HD))).then_inc(sem("lam_in"), 16)
        pool.dma_start(sub_g, a["diff_subln_g"][0:1, :].to_broadcast((P, P))).then_inc(sem("lam_in"), 16)
        for l in range(2):
            if l:
                stage_rows(2)
            stage_rows(2 * l + 1)
            pool.wait_ge(sem("x_done"), 2 * l + 1)
            pool.dma_start(r_w[:, :, 0:NG], a["router_group_w"][l].rearrange("(p t) n -> p t n", t=KT)).then_inc(sem("pool_weights"), 16)
            pool.dma_start(r_w[:, :, NG:], a["router_expert_w"][l].rearrange("(p t) n -> p t n", t=KT)).then_inc(sem("pool_weights"), 16)
            pool.dma_start(r_b[:, 0:NG], a["router_group_b"][l:l + 1, :].to_broadcast((P, NG))).then_inc(sem("pool_weights"), 16)
            pool.dma_start(r_b[:, NG:NG + NX], a["router_expert_b"][l:l + 1].rearrange("a g e -> a (g e)")
                           .to_broadcast((P, NX))).then_inc(sem("pool_weights"), 16)
            with pool.Fori(0, NG) as g:
                for u in range(NE):
                    store_unit(u, g, NX * (l + 1) + g * NE + u + 1, first_dst(1, u, g) if l == 0 else second_dst(u, g),
                               1 if l == 0 else 2)
        pool.wait_ge(sem("h_done"), 4)
        row_load(3, a["final_norm_g"].rearrange("(a n) -> a n", a=1).to_broadcast((P, D)))
        for par in range(2):
            pool.wait_ge(sem(f"ada_out{par}"), 16 * (1 + 16 + 32))
        pool_second(pool)

    def stick_act(act, link, copy):
        act.preload_act_table_set("natural_log_exp_and_others")
        for k in range(HEADS_S + 2):
            if k < HEADS_S:
                act.wait_ge(sem("s_z"), k + 1)
                t, e_ = sb_t[:, k % 2, :], sb_e[:, k % 2, :]
                if k >= 2:
                    act.wait_ge(sem("s_sp"), k - 1)
                link(nc.scalar.activation(t, bank[k % 3][:, 0:384], ACT.Abs))
                link(nc.scalar.activation(t, t, ACT.Exp, scale=-1.0))
                nc.scalar.activation(e_, t, ACT.Ln, bias=1.0).then_inc(sem("s_ln"), 1)
            if 1 <= k <= HEADS_S:
                j = k - 1
                act.wait_ge(sem("s_log"), j + 1)
                nc.scalar.activation(sb_a[:, j % 2, :], sb_a[:, j % 2, :], ACT.Exp).then_inc(sem("s_a"), 1)
            if k >= 2 and k % 2 == 1:
                c = (k - 3) // 2
                act.wait_ge(sem("s_pv"), 2 * c + 2)
                copy(oT[:, c, :], bank[3 + c % 2][:, 0:S]).then_inc(sem("oT"), 1)

    @block.scalar
    def _(act):
        link = Chain(act, sem("act_step"))
        copy = lambda o_, i_: nc.scalar.activation(o_, i_, ACT.Copy)

        def square_norm(n):
            for t in range(TT):
                if n:
                    act.wait_ge(sem("x_done" if t else "x_half"), n)
                else:
                    act.wait_ge(sem("x_in"), 16)
                link(nc.scalar.activation(h[:, t, :], x[:, t, :], ACT.Square, accum_out=ss[:, t:t + 1]))
            act.wait_ge(sem("eps"), 1)
            nc.scalar.activation(ss, ss, ACT.Sqrt, scale=1.0 / D, bias=small[:, 40:41]).then_inc(sem("rms"), 1)

        def take_hT(n):
            for j in range(4):
                act.wait_ge(sem("hT_mm"), 4 * n + j + 1)
                copy(hT[:, 2 * j:2 * j + 2, :], bank[j][:].rearrange("p (t s) -> p t s", t=2)).then_inc(sem("hT_done"), 1)

        def take_qkv(l):
            if l == 0:
                for half in range(2):
                    act.wait_ge(sem(f"ada_out{half}"), 16)
            for i in range(12):
                act.wait_ge(sem("qkv_mm"), EACH["qkv_mm"] * l + i + 1)
                src = bank[i % 4][:]
                if i < 8:
                    dst = (qT, kT)[i // 4][:, 2 * (i % 4):2 * (i % 4) + 2, :]
                    ins = nc.scalar.activation(dst, src.rearrange("p (c s) -> p c s", c=2), ACT.Copy,
                                               scale=HD ** -0.5 if i < 4 else 1.0)
                else:
                    ins = copy(v[:, (i - 8) // 2, (i % 2) * 512:(i % 2 + 1) * 512], src)
                ins.then_inc(sem("qkv"), 1)

        def diff_exp(u):
            nk = P if u % 2 == 0 else S
            act.wait_ge(sem("d_scores"), u + 1)
            for m in range(2):
                c = 2 * (u % 3) + m
                nc.scalar.activation(sc_[u % 3][:, m, 0:nk], sc_[u % 3][:, m, 0:nk], ACT.Exp,
                                     bias=small[:, 48 + c:49 + c], accum_out=small[:, 56 + c:57 + c]).then_inc(sem("d_exp"), 1)

        def diff_awT(u):
            n = 1 + u % 2
            act.wait_ge(sem("d_tr"), u + 1)
            copy(awT[u % 3][:, 0:n, :], bank[6][:, 0:n * P].rearrange("p (k q) -> p k q", k=n)).then_inc(sem("d_awT"), 1)

        def take_oT(l):
            for j in range(4):
                act.wait_ge(sem("oT_mm"), j + 1)
                copy(oT[:, 2 * j:2 * j + 2, :], bank[j][:].rearrange("p (t s) -> p t s", t=2)).then_inc(sem("oT"), 1)

        def experts(l):
            mb = M_BASE[l]
            act.sem_inc(sem("acc"), 1)

            def take_rows(n):
                act.wait_ge(sem("gather_mm"), EACH["gather_mm"] * l + n)
                for k in range(2):
                    copy(hcur[:, 4 * k:4 * k + 4, :], bank[k].rearrange("p (t s) -> p t s", t=4)).then_inc(sem("hcur"), 1)

            take_rows(1)
            act.wait_ge(sem("hover_mm"), EACH["hover_mm"] * l + 1)
            for k in range(2):
                copy(hover[:, 4 * k:4 * k + 4, :], bank[4 + 3 * k][:].rearrange("p (t s) -> p t s", t=4)).then_inc(
                    sem("hover"), 1)
            act.wait_ge(sem("wsl_mm"), EACH["wsl_mm"] * l + 1)
            copy(wsl, bank[5][:, 0:2 * NX]).then_inc(sem("wsl"), 1)
            act.wait_ge(sem("cnt"), EACH["cnt"] * l + 1)
            act.preload_act_table(ACT.Silu)
            with act.Fori(0, NG) as g:
                n_g = act.value_load(cnt[0:1, bass.ds(g, 1)], min_val=0, max_val=S)

                def silu(e):
                    act.wait_ge(sem("gu"), EACH["gu"] * l + g * NE + e + 1)
                    nc.scalar.activation(s_act, bank[2 * (e % 2)][:], ACT.Silu).then_inc(sem("silu"), 1)

                def take_hid(e):
                    act.wait_ge(sem("hid_tr"), EACH["hid_tr"] * l + g * NE + e + 1)
                    copy(hidT, bank[4][:].rearrange("p (t s) -> p t s", t=FK)).then_inc(sem("hidT"), 1)

                for e in range(NE):
                    if e:
                        take_hid(e - 1)
                    silu(e)
                    with act.If(n_g > P):
                        act.wait_ge(sem(f"o_gu{l}"), e + 1)
                        act.wait_ge(sem("hid"), EACH["hid"] * l + g * NE + e + 1)
                        nc.scalar.activation(s_act, bank[2 * ((e + 1) % 2)][:], ACT.Silu).then_inc(sem(f"o_silu{l}"), 1)
                        act.wait_ge(sem(f"o_tr{l}"), e + 1)
                        copy(hidT, bank[4][:].rearrange("p (t s) -> p t s", t=FK)).then_inc(sem(f"o_hidT{l}"), 1)
                    with act.Else():
                        act.sem_inc(free(mb + 3 * e), 1)
                        act.sem_inc(free(mb + 3 * e + 1), 1)
                take_rows(g + 2)
                take_hid(NE - 1)
                n = mb + 3 * NE - 1
                act.wait_ge(free(n), n // RING + 1 + 4 * g)
                for k in range(2):
                    copy(acc[:, bass.ds(g, 1), 512 * k:512 * k + 512].rearrange("p g n -> p (g n)"),
                         bank[5 + k][:]).then_inc(sem("acc"), 1)
            act.wait_ge(sem("hcur"), EACH["hcur"] * (l + 1))
            for k in range(3):
                act.wait_ge(sem("selT_mm"), EACH["selT_mm"] * l + k + 1)
                w = min(512, (NG + 1) * S - 512 * k)
                flat = selT.rearrange("p g s -> p (g s)")
                copy(flat[:, 512 * k:512 * k + w], bank[5 + k][:, 0:w]).then_inc(sem("selT"), 1)

        act.wait_ge(sem("cond_in"), 64)
        nc.scalar.activation(cond, cond, ACT.Silu).then_inc(sem("cond"), 1)
        for l in range(2):
            square_norm(2 * l)
            take_hT(2 * l)
            take_qkv(l)
            if l == 0:
                act.wait_ge(sem("lam_dot"), 1)
                nc.scalar.activation(lvec[:, 2:4], lvec[:, 0:2], ACT.Exp).then_inc(sem("lam_exp"), 1)
                for k in range(16 + 3):
                    if k < 16:
                        diff_exp(k)
                    if k >= 3:
                        diff_awT(k - 3)
                act.wait_ge(sem("sub_ss"), 1)
                nc.scalar.activation(small[:, 80:96], small[:, 64:80], ACT.Sqrt, scale=1.0 / P,
                                     bias=small[:, 41:42]).then_inc(sem("sub_rms"), 1)
                take_oT(l)
            else:
                stick_act(act, link, copy)
            square_norm(2 * l + 1)
            take_hT(2 * l + 1)
            act.wait_ge(sem("gdiff"), EACH["gdiff"] * l + 1)
            nc.scalar.activation(eg, g4c, ACT.Exp).then_inc(sem("r_exp"), 1)
            act.wait_ge(sem("ediff"), EACH["ediff"] * l + 1)
            nc.scalar.activation(ex, den, ACT.Exp).then_inc(sem("r_exp"), 1)
            experts(l)
        stream_rms(act, link, 0, 0)
        square_norm(4)
        act_second(act, link, copy)

    @block.vector
    def _(dve):
        link = Chain(dve, sem("dve_step"))
        V = nc.vector

        def ada_math(l, g, u, conds):
            dve.wait_ge(sem(f"ada_in{u % 2}"), 32 * (16 * l + g * 4 + u // 2 + 1))
            before = NX * l + (g * NE + u) * len(conds)
            for k, c in enumerate(conds):
                w = ada_w[:, u % 2, :].rearrange("p (t n) -> p t n", t=KT)
                prod = ada_prod.rearrange("p (t n) -> p t n", t=KT)
                V.tensor_tensor(prod, w, cond[:, c, :].unsqueeze(2).to_broadcast((P, KT, UC)), ALU.mult).then_inc(sem("ada_mul"), 1)
                dve.wait_ge(sem("ada_mul"), before + k + 1)
                V.tensor_reduce(ada_acc[:, u % 2, k * UC:(k + 1) * UC], ada_prod.rearrange("p (t n) -> p n t", t=KT),
                                AX.X, ALU.add).then_inc(sem("ada_sum"), 1)
                dve.wait_ge(sem("ada_sum"), before + k + 1)

        def ada_take(l, g, u, nconds):
            dve.wait_ge(sem("ada_mm"), NX * (l + 1) + g * NE + u + 1)
            dve.wait_ge(sem(f"ada_out{u % 2}"), 16 * (1 + 16 * l + (g * 4 + u // 2) * nconds))
            for k in range(nconds):
                ins = V.tensor_tensor(ada_row[0:1, u % 2, k * UC:(k + 1) * UC], bank[7][0:1, k * UC:(k + 1) * UC],
                                      ada_bias[0:1, u % 2, :], ALU.add)
            ins.then_inc(sem("ada_row"), 1)

        def norm_rows(n):
            dve.wait_ge(sem("rows_in"), 64 * (n + 1))
            link(V.scalar_tensor_tensor(rows[:, 0, :], rows[:, 0, :], 1.0, rows[:, 3, :], ALU.add, ALU.mult))
            dve.wait_ge(sem("rms"), n + 1)
            link(V.reciprocal(rstd, ss))
            for t in range(TT):
                link(V.scalar_tensor_tensor(h[:, t, :], x[:, t, :], rstd[:, t:t + 1], rows[:, 0, :], ALU.mult, ALU.mult))
            link(V.tensor_tensor(h[:, 0, :], h[:, 0, :], rows[:, 1, :], ALU.add))
            V.tensor_tensor(h[:, 1, :], h[:, 1, :], rows[:, 1, :], ALU.add).then_inc(sem("h_done"), 1)
            dve.wait_ge(sem("h_done"), n + 1)

        def update_x(n, name, scr):
            gate = rows[:, 2 if n % 2 == 0 else 4, :]
            for i in range(4):
                t, hf = i // 2, i % 2
                dve.wait_ge(sem(name), EACH[name] * (n // 2) + i + 1)
                link(V.tensor_tensor(scr[:, t, hf * 512:hf * 512 + 512], bank[i][:], gate[:, hf * 512:hf * 512 + 512], ALU.mult))
                if hf:
                    V.tensor_tensor(x[:, t, :], x[:, t, :], scr[:, t, :], ALU.add).then_inc(sem("x_done" if t else "x_half"), 1)
            dve.wait_ge(sem("x_done"), n + 1)

        def diff_scores(u):
            hd, qt = u // 2, u % 2
            nk = S if qt else P
            dve.wait_ge(sem("d_s"), u + 1)
            s3 = psum[:, 2 * (u % 2):2 * (u % 2) + 2, 0:nk]
            dist = C["dist1" if qt else "dist0"].unsqueeze(1).to_broadcast((P, 2, nk))
            link(V.scalar_tensor_tensor(sc_[u % 3][:, :, 0:nk], dist, 2.0 ** (-(hd + 1)), s3, ALU.mult, ALU.add))
            V.tensor_reduce(small[:, 48 + 2 * (u % 3):50 + 2 * (u % 3)], sc_[u % 3][:, :, 0:nk], AX.X, ALU.max,
                            negate=True).then_inc(sem("d_scores"), 1)
            dve.wait_ge(sem("d_scores"), u + 1)

        def diff_combine(u):
            nk = S if u % 2 else P
            dve.wait_ge(sem("d_exp"), 2 * u + 2)
            if u >= 3:
                dve.wait_ge(sem("d_tr"), u - 2)
            r = small[:, 344 + 2 * (u % 3):346 + 2 * (u % 3)]
            sums = small[:, 56 + 2 * (u % 3):58 + 2 * (u % 3)]
            link(V.reciprocal(r, sums))
            link(V.tensor_scalar(r[:, 1:2], r[:, 1:2], lam, None, ALU.mult))
            link(V.tensor_scalar(aw[u % 3][:, 0:nk], sc_[u % 3][:, 1, 0:nk], r[:, 1:2], None, ALU.mult))
            V.scalar_tensor_tensor(aw[u % 3][:, 0:nk], sc_[u % 3][:, 0, 0:nk], r[:, 0:1], aw[u % 3][:, 0:nk],
                                   ALU.mult, ALU.add).then_inc(sem("d_a"), 1)
            dve.wait_ge(sem("d_a"), u + 1)

        def diff_out(u):
            dve.wait_ge(sem("d_pv"), u + 1)
            V.tensor_copy(o[:, u % 2, (u // 2) * P:(u // 2 + 1) * P], bank[4 + u % 2][:, 0:P]).then_inc(sem("d_o"), 1)

        def router(l):
            bc = lambda t, n_: t.unsqueeze(2).to_broadcast((P, TT, n_))
            dve.wait_ge(sem("pool_weights"), 64 * (l + 1))
            dve.wait_ge(sem("logits"), EACH["logits"] * l + 1)
            logits = bank[0][:, 0:TT * (NG + NX)].rearrange("p (t n) -> p t n", t=TT)
            lg, le = logits[:, :, 0:NG], logits[:, :, NG:]
            link(V.tensor_tensor(g4, lg, r_b[:, 0:NG].unsqueeze(1).to_broadcast((P, TT, NG)), ALU.add))
            link(V.tensor_tensor(e32, le, r_b[:, NG:].unsqueeze(1).to_broadcast((P, TT, NX)), ALU.add))

            def first_max(hot, t_, mx, tmp, prio, n_):
                link(V.tensor_reduce(mx, t_, AX.X, ALU.max))
                link(V.tensor_tensor(tmp, t_, bc(mx, n_), ALU.is_ge))
                link(V.tensor_tensor(tmp, tmp, prio.unsqueeze(1).to_broadcast((P, TT, n_)), ALU.mult))
                link(V.tensor_reduce(pm, tmp, AX.X, ALU.max))
                link(V.tensor_tensor(hot, tmp, bc(pm, n_), ALU.is_equal))

            first_max(og, g4, gm, g4b, C["prio4"], NG)
            V.tensor_tensor(g4c, g4, bc(gm, NG), ALU.subtract).then_inc(sem("gdiff"), 1)
            e4 = e32.rearrange("p t (g e) -> p t g e", g=NG)
            e4b = e32b.rearrange("p t (g e) -> p t g e", g=NG)
            for t in range(TT):
                link(V.tensor_tensor(e4b[:, t], e4[:, t], og[:, t].unsqueeze(2).to_broadcast((P, NG, NE)), ALU.mult))
            link(V.tensor_reduce(e8, e32b.rearrange("p t (g e) -> p t e g", g=NG), AX.X, ALU.add))
            first_max(o1, e8, m1, t8, C["prio8"], NE)
            link(V.scalar_tensor_tensor(e8b, o1, -3e38, e8, ALU.mult, ALU.add))
            first_max(o2, e8b, m2, t8, C["prio8"], NE)
            V.tensor_tensor(den, m2, m1, ALU.subtract).then_inc(sem("ediff"), 1)
            dve.wait_ge(sem("r_exp"), EACH["r_exp"] * l + 2)
            link(V.tensor_reduce(gs, eg, AX.X, ALU.add))
            link(V.tensor_scalar(den, ex, 1.0, None, ALU.add))
            link(V.tensor_tensor(den, den, gs, ALU.mult))
            link(V.reciprocal(w1, den))
            link(V.tensor_tensor(w2, w1, ex, ALU.mult))
            link(V.tensor_tensor(t8, o1, bc(w1, NE), ALU.mult))
            link(V.tensor_tensor(e8b, o2, bc(w2, NE), ALU.mult))
            link(V.tensor_tensor(t8, t8, e8b, ALU.add))
            w4 = w32.rearrange("p t (g e) -> p t g e", g=NG)
            for t in range(TT):
                link(V.tensor_tensor(w4[:, t], t8[:, t].unsqueeze(1).to_broadcast((P, NG, NE)),
                                     og[:, t].unsqueeze(2).to_broadcast((P, NG, NE)), ALU.mult))
            V.tensor_tensor(ogs, og[:, 0], og[:, 1], ALU.add).then_inc(sem("og"), 1)
            dve.wait_ge(sem("rank_mm"), EACH["rank_mm"] * l + 1)
            rank = bank[2][:, 0:TT * NG].rearrange("p (t g) -> p t g", t=TT)
            link(V.tensor_tensor(rkt, rank, og, ALU.mult))
            link(V.tensor_reduce(rk, rkt, AX.X, ALU.add))
            V.tensor_copy(cnt[0:1, 0:NG], bank[2][0:1, TT * NG:TT * NG + NG]).then_inc(sem("cnt"), 1)
            for t in range(TT):
                for g in range(NG):
                    link(V.tensor_scalar(sel[:, t, g, :], C["iota"], rk[:, t:t + 1], og[:, t, g:g + 1], ALU.is_equal, ALU.mult))
                ins = V.tensor_scalar(sel[:, t, NG, :], C["iota_over"], rk[:, t:t + 1], None, ALU.is_equal)
                ins.then_inc(sem("sel"), 1)
            dve.wait_ge(sem("sel"), EACH["sel"] * l + TT)

        def experts(l):
            dve.wait_ge(sem("wsl"), EACH["wsl"] * l + 1)
            link(V.memset(acc[:, NG, :], 0.0))
            dve.wait_ge(sem("cnt"), EACH["cnt"] * l + 1)
            conds = [0] if l == 0 else [1, 2]
            with dve.Fori(0, NG) as g:
                n_g = dve.value_load(cnt[0:1, bass.ds(g, 1)], min_val=0, max_val=S)
                for e in range(NE):
                    ada_math(l, g, e, conds)
                    ada_take(l, g, e, len(conds))
                    dve.wait_ge(sem("silu"), EACH["silu"] * l + g * NE + e + 1)
                    V.scalar_tensor_tensor(hid, s_act, wsl[:, bass.ds(g * NE + e, 1)], bank[2 * (e % 2) + 1][:],
                                           ALU.mult, ALU.mult).then_inc(sem("hid"), 1)
                    with dve.If(n_g > P):
                        dve.wait_ge(sem(f"o_silu{l}"), e + 1)
                        V.scalar_tensor_tensor(s_act, s_act, wsl[:, bass.ds(g * NE + e + NX, 1)],
                                               bank[2 * ((e + 1) % 2) + 1][:], ALU.mult, ALU.mult).then_inc(sem(f"o_hid{l}"), 1)
                        dve.wait_ge(sem(f"o_down{l}"), e + 1)
                        for k in range(2):
                            V.tensor_tensor(acc[:, NG, 512 * k:512 * k + 512], acc[:, NG, 512 * k:512 * k + 512],
                                            bank[2 * ((e + 1) % 2) + k][:], ALU.add).then_inc(sem(f"o_add{l}"), 1)
                        dve.wait_ge(sem(f"o_add{l}"), 2 * e + 2)

        link(V.memset(small[:, 40:41], 1e-6))
        V.memset(small[:, 41:42], 1e-5).then_inc(sem("eps"), 1)
        dve.wait_ge(sem("consts"), 16)
        dve.wait_ge(sem("cond"), 1)
        for n in range(NX):
            dve.wait_ge(sem("ada_mm"), n + 1)
            part = bias0[:, n * UC:(n + 1) * UC]
            V.tensor_tensor(part, bank[6 + n % 2][0:1, 0:UC], part, ALU.add).then_inc(sem("ada_row"), 1)
            if n == NX * 3 // 4:
                norm_rows(0)
        for l in range(2):
            if l:
                norm_rows(2)
            if l == 0:
                dve.wait_ge(sem("lam_in"), 16 * 5)
                link(V.tensor_tensor(lqk[:, 0:4:2, :], lqk[:, 0:4:2, :], lqk[:, 1:4:2, :], ALU.mult))
                V.tensor_reduce(lvec[:, 0:2], lqk[:, 0:4:2, :], AX.X, ALU.add).then_inc(sem("lam_dot"), 1)
                dve.wait_ge(sem("lam_exp"), 1)
                link(V.tensor_tensor(lam, lvec[:, 3:4], lvec[:, 2:3], ALU.subtract))
                link(V.tensor_scalar(lam, lam, -0.2, None, ALU.add))
                for k in range(16 + 4):
                    if k < 16:
                        diff_scores(k)
                    if 2 <= k < 18:
                        diff_combine(k - 2)
                    if k >= 4:
                        diff_out(k - 4)
                dve.wait_ge(sem("d_o"), 16)
                o4 = o.rearrange("p t (h e) -> p (t h) e", h=HEADS_D)
                sq = qT.rearrange("p a b -> p (a b)").rearrange("p (g e) -> p g e", e=P)
                link(V.tensor_tensor(sq, o4, o4, ALU.mult))
                V.tensor_reduce(small[:, 64:80], sq, AX.X, ALU.add).then_inc(sem("sub_ss"), 1)
                dve.wait_ge(sem("sub_rms"), 1)
                link(V.reciprocal(small[:, 80:96], small[:, 80:96]))
                link(V.tensor_scalar(sub_g, sub_g, 0.8, None, ALU.mult))
                link(V.tensor_tensor(o4, o4, small[:, 80:96].unsqueeze(2).to_broadcast((P, 16, P)), ALU.mult))
                V.tensor_tensor(o4, o4, sub_g.unsqueeze(1).to_broadcast((P, 16, P)), ALU.mult).then_inc(sem("sub_done"), 1)
                dve.wait_ge(sem("sub_done"), 1)
            else:
                link(V.tensor_scalar(hide, C["strict"], 1.0, -NBIG, ALU.subtract, ALU.mult))
                for k in range(HEADS_S + 1):
                    if k < HEADS_S:
                        dve.wait_ge(sem("s_ln"), k + 1)
                        if k >= 2:
                            dve.wait_ge(sem("s_c"), k - 1)
                        link(V.scalar_tensor_tensor(sb_sp[:, k % 2, :], bank[k % 3][:, 0:384], 0.0, sb_e[:, k % 2, :],
                                                    ALU.max, ALU.add))
                        V.tensor_tensor(sb_sp[:, k % 2, :], sb_sp[:, k % 2, :], C["strict"], ALU.mult).then_inc(sem("s_sp"), 1)
                    if k >= 1:
                        j = k - 1
                        dve.wait_ge(sem("s_c"), j + 1)
                        if j >= 2:
                            dve.wait_ge(sem("s_pv"), j - 1)
                        V.scalar_tensor_tensor(sb_a[:, j % 2, :], bank[j % 3][:, 0:384], 0.0, hide,
                                               ALU.min, ALU.add).then_inc(sem("s_log"), 1)
            update_x(2 * l, "proj_mm", v)
            norm_rows(2 * l + 1)
            router(l)
            experts(l)
            update_x(2 * l + 1, "y_mm", h)
        stream_norm(dve, link, 0, 0)
        dve.wait_ge(sem("rows_in"), 16 * 17)
        dve.wait_ge(sem("rms"), 6)
        link(V.reciprocal(rstd, ss))
        link(V.scalar_tensor_tensor(x[:, 0, :], x[:, 0, :], rstd[:, 0:1], rows[:, 3, :], ALU.mult, ALU.mult))
        V.scalar_tensor_tensor(x[:, 1, :], x[:, 1, :], rstd[:, 1:2], rows[:, 3, :], ALU.mult, ALU.mult).then_inc(sem("x_done"), 1)
        dve.wait_ge(sem("x_done"), 5)
        dve_second(dve, link)

    @block.tensor
    def _(pe):
        T = nc.tensor

        def mm(out_, lhsT, rhs, start, stop):
            return T.matmul(out_, lhsT, rhs, start=start, stop=stop, skip_group_check=True)

        def transpose_h(n):
            pe.wait_ge(sem("h_done"), n + 1)
            for j in range(4):
                for i in range(4):
                    t, tile = 2 * j + i // 2, i % 2
                    ins = T.transpose(bank[j][:, i * P:(i + 1) * P], h[:, tile, t:D:KT], ident)
                ins.then_inc(sem("hT_mm"), 1)

        def qkv(l):
            b = L_BASE[l]
            pe.wait_ge(sem("hT_done"), 8 * l + 4)
            for i in range(12):
                n = b + (i // 2 if i < 8 else 4 + i % 2)
                if i < 10:
                    loaded(pe, n)
                if i >= 4:
                    pe.wait_ge(sem("qkv"), EACH["qkv"] * l + i - 3)
                w = wslot(n, KT, 512)
                if i < 8:
                    for c in range(2):
                        for t in range(KT):
                            col = (i % 2) * 256 + c * P
                            ins = mm(bank[i % 4][:, c * S:(c + 1) * S], w[:, t, col:col + P], hT[:, t, :], t == 0, t == KT - 1)
                    if i % 2:
                        ins.then_inc(free(n), 1)
                        pe.wait_ge(free(n), n // RING + 1)
                        pe.sem_inc(sem("qkv_mm"), 1)
                    else:
                        ins.then_inc(sem("qkv_mm"), 1)
                else:
                    tile = (i - 8) // 2
                    for t in range(KT):
                        ins = mm(bank[i % 4][:], hT[:, t, tile * P:(tile + 1) * P], w[:, t, :], t == 0, t == KT - 1)
                    if tile:
                        ins.then_inc(free(n), 1)
                        pe.wait_ge(free(n), n // RING + 1)
                        pe.sem_inc(sem("qkv_mm"), 1)
                    else:
                        ins.then_inc(sem("qkv_mm"), 1)

        def projection(l):
            b = L_BASE[l]
            for hf in range(2):
                loaded(pe, b + 6 + hf)
            for i in range(4):
                tile, hf = i // 2, i % 2
                w = wslot(b + 6 + hf, KT, 512)
                for t in range(KT):
                    ins = mm(bank[i][:], oT[:, t, tile * P:(tile + 1) * P], w[:, t, :], t == 0, t == KT - 1)
                ins.then_inc(sem("proj_mm"), 1)
            for hf in range(2):
                pe.wait_ge(sem("proj_mm"), EACH["proj_mm"] * l + 4)
                pe.sem_inc(free(b + 6 + hf), 1)

        def diff_attention():
            pe.wait_ge(sem("qkv"), 12)
            for k in range(16 + 4):
                if k < 16:
                    hd, qt = k // 2, k % 2
                    nk = S if qt else P
                    if k >= 2:
                        pe.wait_ge(sem("d_scores"), k - 1)
                    for m in range(2):
                        lo = m * HD
                        ins = mm(bank[2 * (k % 2) + m][:, 0:nk], qT[lo:lo + HD, hd, qt * P:(qt + 1) * P],
                                 kT[lo:lo + HD, hd, 0:nk], True, True)
                    ins.then_inc(sem("d_s"), 1)
                if 3 <= k < 19:
                    u = k - 3
                    pe.wait_ge(sem("d_a"), u + 1)
                    if u:
                        pe.wait_ge(sem("d_awT"), u)
                    for j in range(1 + u % 2):
                        ins = T.transpose(bank[6][:, j * P:(j + 1) * P], aw[u % 3][:, j * P:(j + 1) * P], ident)
                    ins.then_inc(sem("d_tr"), 1)
                if k >= 4:
                    u = k - 4
                    hd = u // 2
                    pe.wait_ge(sem("d_awT"), u + 1)
                    if u >= 2:
                        pe.wait_ge(sem("d_o"), u - 1)
                    n = 1 + u % 2
                    for j in range(n):
                        ins = mm(bank[4 + u % 2][:, 0:P], awT[u % 3][:, j, :], v[:, j, hd * P:(hd + 1) * P],
                                 j == 0, j == n - 1)
                    ins.then_inc(sem("d_pv"), 1)
            pe.wait_ge(sem("sub_done"), 1)
            for j in range(4):
                for i in range(4):
                    t, tile = 2 * j + i // 2, i % 2
                    ins = T.transpose(bank[j][:, i * P:(i + 1) * P], o[:, tile, t * P:(t + 1) * P], ident)
                ins.then_inc(sem("oT_mm"), 1)
            pe.wait_ge(sem("oT"), 4)

        def stick_attention():
            pe.wait_ge(sem("qkv"), 24)
            for k in range(HEADS_S + 2):
                if k < HEADS_S:
                    c, lo = k // 2, HD * (k % 2)
                    if k >= 3:
                        pe.wait_ge(sem("s_log"), k - 2)
                    b = bank[k % 3]
                    mm(b[:, 0:S], kT[lo:lo + HD, c, 0:P], qT[lo:lo + HD, c, :], True, True)
                    mm(b[:, S:384], kT[lo:lo + HD, c, P:S], qT[lo:lo + HD, c, P:S], False, True).then_inc(sem("s_z"), 1)
                if 1 <= k <= HEADS_S:
                    j = k - 1
                    b, s = bank[j % 3], sb_sp[:, j % 2, :]
                    pe.wait_ge(sem("s_sp"), j + 1)
                    mm(b[:, 0:S], C["suffix"], s[:, 0:S], False, True)
                    mm(b[:, P:S], C["minus"], s[:, S:384], False, True)
                    mm(b[:, S:384], C["suffix"], s[:, S:384], False, True).then_inc(sem("s_c"), 1)
                if k >= 2:
                    j = k - 2
                    c, lo = j // 2, HD * (j % 2)
                    b = bank[3 + c % 2]
                    pe.wait_ge(sem("s_a"), j + 1)
                    if c >= 2:
                        pe.wait_ge(sem("oT"), 4 + c - 1)
                    hd = slice(j * HD, (j + 1) * HD)
                    mm(b[lo:lo + HD, 0:S], v[:, 0, hd], sb_a[:, j % 2, 0:S], True, False)
                    mm(b[lo:lo + HD, P:S], v[:, 1, hd], sb_a[:, j % 2, S:384], False, True).then_inc(sem("s_pv"), 1)
            pe.wait_ge(sem("oT"), 12)

        def router(l):
            pe.wait_ge(sem("hT_done"), 8 * l + 8)
            pe.wait_ge(sem("pool_weights"), 64 * (l + 1))
            for tile in range(TT):
                for t in range(KT):
                    lhs = hT[:, t, tile * P:(tile + 1) * P]
                    ins = mm(bank[0][:, tile * (NG + NX):(tile + 1) * (NG + NX)], lhs, r_w[:, t, :], t == 0, t == KT - 1)
            ins.then_inc(sem("logits"), 1)
            pe.wait_ge(sem("og"), EACH["og"] * l + 1)
            r = bank[2]
            mm(r[:, 0:NG], C["before"], og[:, 0], True, True)
            mm(r[:, NG:2 * NG], C["ones"], og[:, 0], True, False)
            mm(r[:, NG:2 * NG], C["before"], og[:, 1], False, True)
            mm(r[:, 2 * NG:3 * NG], C["ones"], ogs, True, True).then_inc(sem("rank_mm"), 1)
            pe.wait_ge(sem("sel"), EACH["sel"] * l + TT)
            gather(sel[:, :, 0, :], 0, 1).then_inc(sem("gather_mm"), 1)
            gather(sel[:, :, NG, :], 4, 7).then_inc(sem("hover_mm"), 1)
            for g in range(NG):
                for tile in range(TT):
                    mm(bank[5][:, g * NE:(g + 1) * NE], sel[:, tile, g, :], w32[:, tile, g * NE:(g + 1) * NE], tile == 0, tile == 1)
            for tile in range(TT):
                ins = mm(bank[5][:, NX:2 * NX], sel[:, tile, NG, :], w32[:, tile, :], tile == 0, tile == 1)
            ins.then_inc(sem("wsl_mm"), 1)
            pe.wait_ge(sem("hover"), EACH["hover"] * l + 2)
            pe.wait_ge(sem("wsl"), EACH["wsl"] * l + 1)

        def gather(pick, b0, b1):
            for t in range(KT):
                for tile in range(TT):
                    ins = mm(bank[(b0, b1)[t // 4]][:, (t % 4) * P:(t % 4 + 1) * P], h[:, tile, t:D:KT], pick[:, tile],
                             tile == 0, tile == 1)
            return ins

        def experts(l):
            mb = M_BASE[l]
            nconds = l + 1
            pe.wait_ge(sem("cnt"), EACH["cnt"] * l + 1)
            with pe.Fori(0, NG) as g:
                n_g = pe.value_load(cnt[0:1, bass.ds(g, 1)], min_val=0, max_val=S)
                pe.wait_ge(sem("hcur"), EACH["hcur"] * l + 2 * g + 2)

                def gate_up(e, j, t0, t1, who, b):
                    w = wslot(mb + 3 * e + j, KT, 512)
                    for t in range(t0, t1):
                        ins = mm(bank[b + j][:], who[:, t, :], w[:, t, :], t == 0, t == KT - 1)
                    return ins

                def turn(src, b_sem):
                    for t in range(FK):
                        ins = T.transpose(bank[4][:, t * P:(t + 1) * P], src[:, t:FH:FK], ident)
                    ins.then_inc(b_sem, 1)

                def down(e, b0, first, last_):
                    w = ring[:, slot(mb + 3 * e + 2), :].rearrange("p (t n) -> p t n", t=FK)
                    for t in range(FK):
                        for k in range(2):
                            ins = mm(bank[b0 + k][:], hidT[:, t, :], w[:, t, k * 512:(k + 1) * 512], first and t == 0, last_ and t == FK - 1)
                    return ins

                for e in range(NE + 1):
                    b = 2 * (e % 2)
                    if e < NE:
                        loaded(pe, mb + 3 * e, g)
                        gate_up(e, 0, 0, KT, hcur, b)
                    else:
                        gather(sel[:, :, bass.ds(g + 1, 1), :].rearrange("p t g s -> p t (g s)"), 0, 1).then_inc(
                            sem("gather_mm"), 1)
                    if e:
                        pe.wait_ge(sem("hid"), EACH["hid"] * l + g * NE + e)
                        turn(hid, sem("hid_tr"))
                    if e < NE:
                        loaded(pe, mb + 3 * e + 1, g)
                        gate_up(e, 1, 0, KT - 1, hcur, b)
                    if e < NE:
                        pe.wait_ge(sem("ada_row"), NX * (l + 1) + g * NE + e)
                        pe.wait_ge(sem("ada_sum"), NX * l + (g * NE + e + 1) * nconds)
                        mm(bank[7][0:1, 0:nconds * UC], C["ones"][:, 0:1], ada_acc[:, e % 2, 0:nconds * UC], True, True).then_inc(
                            sem("ada_mm"), 1)
                    if e:
                        if e == 1:
                            pe.wait_ge(sem("acc"), EACH["acc"] * l + 2 * g + 1)
                        loaded(pe, mb + 3 * (e - 1) + 2, g)
                        pe.wait_ge(sem("hidT"), EACH["hidT"] * l + g * NE + e)
                        down(e - 1, 5, e == 1, e == NE).then_inc(free(mb + 3 * (e - 1) + 2), 1)
                    if e < NE:
                        gate_up(e, 1, KT - 1, KT, hcur, b).then_inc(sem("gu"), 1)
                        with pe.If(n_g > P):
                            ob = 2 * ((e + 1) % 2)
                            gate_up(e, 0, 0, KT, hover, ob).then_inc(free(mb + 3 * e), 1)
                            gate_up(e, 1, 0, KT, hover, ob).then_inc(free(mb + 3 * e + 1), 1)
                            pe.wait_ge(free(mb + 3 * e + 1), (mb + 3 * e + 1) // RING + 1 + 4 * g)
                            pe.sem_inc(sem(f"o_gu{l}"), 1)
                            pe.wait_ge(sem(f"o_hid{l}"), e + 1)
                            turn(s_act, sem(f"o_tr{l}"))
                            loaded(pe, mb + 3 * e + 2, g)
                            pe.wait_ge(sem(f"o_hidT{l}"), e + 1)
                            down(e, ob, True, True).then_inc(sem(f"o_down{l}"), 1)
                            pe.wait_ge(sem(f"o_add{l}"), 2 * e + 2)
            pe.wait_ge(sem("acc"), EACH["acc"] * (l + 1))
            pe.wait_ge(sem("ada_row"), NX * (l + 2))
            for i in range(2 * (NG + 1)):
                g, tile = i // 2, i % 2
                ins = T.transpose(bank[5 + i // 4][:, (i % 4) * P:(i % 4 + 1) * P], sel[:, tile, g, :], ident)
                if i % 4 == 3 or i == 2 * NG + 1:
                    ins.then_inc(sem("selT_mm"), 1)
            pe.wait_ge(sem("selT"), EACH["selT"] * l + 3)
            for i in range(4):
                tile, hf = i // 2, i % 2
                for g in range(NG + 1):
                    ins = mm(bank[i][:], selT[:, g, tile * P:(tile + 1) * P], acc[:, g, hf * 512:hf * 512 + 512], g == 0, g == NG)
                ins.then_inc(sem("y_mm"), 1)

        pe.wait_ge(sem("consts"), 16)
        pe.wait_ge(sem("cond"), 1)
        for n in range(NX):
            pe.wait_ge(sem(f"start_in{n % AB}"), 16 * (n // AB + 1))
            if n >= 2:
                pe.wait_ge(sem("ada_row"), n - 1)
            for t in range(KT):
                ins = mm(bank[6 + n % 2][0:1, 0:UC], cond[:, 0, t:t + 1], ada0[:, n % AB, t, :], t == 0, t == KT - 1)
            ins.then_inc(sem("ada_mm"), 1)
        for l in range(2):
            transpose_h(2 * l)
            qkv(l)
            (diff_attention, stick_attention)[l]()
            projection(l)
            transpose_h(2 * l + 1)
            router(l)
            experts(l)
        pe_second(pe, mm)


NAMES = (
    "x", "c", "norm1_g", "norm2_g", "ada_w", "ada_b", "diff_w_in", "diff_w_out", "diff_lambda_q1", "diff_lambda_k1",
    "diff_lambda_q2", "diff_lambda_k2", "diff_subln_g", "sb_w_in", "sb_w_out", "router_group_w", "router_group_b",
    "router_expert_w", "router_expert_b", "expert_w_gate", "expert_w_up", "expert_w_down", "final_norm_g", "c_2", "ctx_2",
    "c_ctx_2", "w_mod_2", "b_mod_2", "norm_g_2", "w_in_2", "w_fmix_2", "g_ln_g_2", "g_ws_2", "g_bs_2", "q_a_g_2", "w_uq_2",
    "kv_a_g_2", "w_ukv_2", "q_norm_g_2", "k_norm_g_2", "w_out_2",
)


def kernel(**inputs):
    import concourse.bacc as bacc
    from concourse.bass_utils import run_bass_kernel_spmd

    nc = bacc.Bacc("TRN2", target_bir_lowering=False, num_devices=1)
    arrays = {n: np.ascontiguousarray(inputs[n]) for n in NAMES}
    arrays.update(constants())
    a = {n: nc.dram_tensor("in_" + n, v.shape, mybir.dt.from_np(v.dtype), kind="ExternalInput").ap() for n, v in arrays.items()}
    out = nc.dram_tensor("out_x", (1, S, D), F32, kind="ExternalOutput").ap()
    build(nc, a, out)
    r = run_bass_kernel_spmd(nc, [{"in_" + n: v for n, v in arrays.items()}], core_ids=[0])
    return r.results[0]["out_x"]
```
